# Optimizing a Trainium2 kernel written in Bass

```python
import math
import jax, jax.numpy as jnp
from jax import lax
import numpy as np

D_MODEL = 2048
BATCH = 1
SEQ = 256
DEPTH = 1

HEAD_DIM = 64
N_HEADS = D_MODEL // 256
ATTN_WIDTH = N_HEADS * 2 * HEAD_DIM
POOL_WINDOWS = (2, 4, 8, 16)
N_POOL_GROUPS = len(POOL_WINDOWS)
POOL_WIDTH = D_MODEL // 2
POOL_GROUP_DIM = POOL_WIDTH // N_POOL_GROUPS
N_BRANCH = 2
IN_COLS = 3 * ATTN_WIDTH + POOL_WIDTH + N_BRANCH * D_MODEL
D_FF = (11 * D_MODEL // 4) // 128 * 128
CONV_WIDTH = 3
Q_BLOCK = 128
NORM_EPS = 1e-6
SUBLN_EPS = 1e-5

kernel_name = 'hybrid_diffattn_pool_convffn_block'

def rms_norm(x, g, eps=NORM_EPS):
    xf = x.astype(jnp.float32)
    y = xf * lax.rsqrt(jnp.mean(xf * xf, axis=-1, keepdims=True) + eps)
    return (y * g.astype(jnp.float32)).astype(x.dtype)

def alibi_slopes():
    return jnp.asarray(np.array([2.0 ** (-8.0 * (h + 1) / N_HEADS) for h in range(N_HEADS)], dtype=np.float32))

def diff_attention(q, k, v, lam, slopes):
    B, S = q.shape[0], q.shape[1]
    nb = S // Q_BLOCK
    q_blocks = q.reshape(B, nb, Q_BLOCK, N_HEADS, 2, HEAD_DIM).transpose(1, 0, 2, 3, 4, 5)
    starts = jnp.arange(nb, dtype=jnp.int32) * Q_BLOCK
    key_pos = jnp.arange(S, dtype=jnp.int32)
    scale = HEAD_DIM ** -0.5

    def one_block(args):
        qb, start = args
        s = jnp.einsum('bqhcd,bkhcd->bhcqk', qb, k).astype(jnp.float32) * scale
        q_pos = start + jnp.arange(Q_BLOCK, dtype=jnp.int32)
        dist = jnp.abs(q_pos[:, None] - key_pos[None, :]).astype(jnp.float32)
        s = s - slopes[None, :, None, None, None] * dist[None, None, None]
        p = jax.nn.softmax(s, axis=-1)
        a = p[:, :, 0] - lam * p[:, :, 1]
        return jnp.einsum('bhqk,bkhe->bqhe', a.astype(v.dtype), v)

    out = lax.map(one_block, (q_blocks, starts))
    return out.transpose(1, 0, 2, 3, 4).reshape(B, S, N_HEADS, 2 * HEAD_DIM)

def pool_mixer(p, pool_w, pool_scale):
    B, S, _ = p.shape
    pg = p.reshape(B, S, N_POOL_GROUPS, POOL_GROUP_DIM)
    pf = pg.astype(jnp.float32)
    csum = jnp.pad(jnp.cumsum(pf, axis=1), ((0, 0), (1, 0), (0, 0), (0, 0)))
    t = jnp.arange(S, dtype=jnp.int32)
    halves = jnp.asarray(np.array([w // 2 for w in POOL_WINDOWS], dtype=np.int32))
    lo = jnp.clip(t[None, :] - halves[:, None], 0, S)
    hi = jnp.clip(t[None, :] + halves[:, None], 0, S)
    cnt = (hi - lo).astype(jnp.float32)
    c_g = csum.transpose(2, 0, 1, 3)
    take = jax.vmap(lambda cg, idx: cg[:, idx])
    win_sum = take(c_g, hi) - take(c_g, lo)
    mean = win_sum / cnt[:, None, :, None]
    mixed = (mean.transpose(1, 2, 0, 3) - pf).astype(p.dtype)
    y = jnp.einsum('bsgc,gcd->bsgd', mixed, pool_w)
    y = y * pool_scale.reshape(N_POOL_GROUPS, POOL_GROUP_DIM)
    return y.reshape(B, S, POOL_WIDTH)

def depthwise_conv_centred(u, w, b):
    up = jnp.pad(u, ((0, 0), (1, 1), (0, 0)))
    return up[:, :-2] * w[0] + up[:, 1:-1] * w[1] + up[:, 2:] * w[2] + b

def setup_inputs(seed: int = 0) -> dict:
    key = jax.random.key(seed)
    ks = jax.random.split(key, 24)
    f = jnp.float32
    L = DEPTH

    def nrm(k, shape, s):
        return jax.random.normal(k, shape, f) * s

    return {
        'x': nrm(ks[0], (BATCH, SEQ, D_MODEL), 1.0),
        'g_pre_mix': 1.0 + nrm(ks[1], (L, D_MODEL), 0.02),
        'w_in': nrm(ks[2], (L, D_MODEL, IN_COLS), D_MODEL ** -0.5),
        'b_gate': nrm(ks[3], (L, N_BRANCH * D_MODEL), 0.02),
        'lambda_q1': nrm(ks[4], (L, HEAD_DIM), 0.1),
        'lambda_k1': nrm(ks[5], (L, HEAD_DIM), 0.1),
        'lambda_q2': nrm(ks[6], (L, HEAD_DIM), 0.1),
        'lambda_k2': nrm(ks[7], (L, HEAD_DIM), 0.1),
        'subln_gain': 1.0 + nrm(ks[8], (L, 2 * HEAD_DIM), 0.02),
        'w_attn_branch': nrm(ks[9], (L, ATTN_WIDTH, D_MODEL), ATTN_WIDTH ** -0.5),
        'pool_w': nrm(ks[10], (L, N_POOL_GROUPS, POOL_GROUP_DIM, POOL_GROUP_DIM), POOL_GROUP_DIM ** -0.5),
        'pool_scale': 1.0 + nrm(ks[11], (L, POOL_WIDTH), 0.02),
        'w_pool_branch': nrm(ks[12], (L, POOL_WIDTH, D_MODEL), POOL_WIDTH ** -0.5),
        'w_out': nrm(ks[13], (L, D_MODEL, D_MODEL), D_MODEL ** -0.5),
        'g_post_mix': 1.0 + nrm(ks[14], (L, D_MODEL), 0.02),
        'g_pre_ffn': 1.0 + nrm(ks[15], (L, D_MODEL), 0.02),
        'w_up': nrm(ks[16], (L, D_MODEL, 2 * D_FF), D_MODEL ** -0.5),
        'conv_w': nrm(ks[17], (L, CONV_WIDTH, 2 * D_FF), CONV_WIDTH ** -0.5),
        'conv_b': nrm(ks[18], (L, 2 * D_FF), 0.02),
        'w_down': nrm(ks[19], (L, D_FF, D_MODEL), D_FF ** -0.5),
        'g_post_ffn': 1.0 + nrm(ks[20], (L, D_MODEL), 0.02),
    }

def reference(x, g_pre_mix, w_in, b_gate, lambda_q1, lambda_k1, lambda_q2, lambda_k2, subln_gain,
              w_attn_branch, pool_w, pool_scale, w_pool_branch, w_out, g_post_mix,
              g_pre_ffn, w_up, conv_w, conv_b, w_down, g_post_ffn):
    B, S, D = x.shape
    slopes = alibi_slopes()
    splits = [ATTN_WIDTH, 2 * ATTN_WIDTH, 3 * ATTN_WIDTH, 3 * ATTN_WIDTH + POOL_WIDTH]
    for l in range(DEPTH):
        lambda_init = 0.8 - 0.6 * math.exp(-0.3 * l)
        h = rms_norm(x, g_pre_mix[l])
        z = h @ w_in[l]
        q, k, v, pz, gz = jnp.split(z, splits, axis=-1)
        q = q.reshape(B, S, N_HEADS, 2, HEAD_DIM)
        k = k.reshape(B, S, N_HEADS, 2, HEAD_DIM)
        v = v.reshape(B, S, N_HEADS, 2 * HEAD_DIM)
        lam = (jnp.exp(jnp.sum(lambda_q1[l].astype(jnp.float32) * lambda_k1[l].astype(jnp.float32)))
               - jnp.exp(jnp.sum(lambda_q2[l].astype(jnp.float32) * lambda_k2[l].astype(jnp.float32)))
               + lambda_init)
        o = diff_attention(q, k, v, lam, slopes)
        o = rms_norm(o, subln_gain[l], SUBLN_EPS) * (1.0 - lambda_init)
        y_attn = o.reshape(B, S, ATTN_WIDTH) @ w_attn_branch[l]
        y_pool = pool_mixer(pz, pool_w[l], pool_scale[l]) @ w_pool_branch[l]
        gates = jax.nn.sigmoid(gz + b_gate[l]).reshape(B, S, N_BRANCH, D)
        merged = gates[:, :, 0] * y_attn + gates[:, :, 1] * y_pool
        x = x + rms_norm(merged @ w_out[l], g_post_mix[l])
        h2 = rms_norm(x, g_pre_ffn[l])
        u = depthwise_conv_centred(h2 @ w_up[l], conv_w[l], conv_b[l])
        gate, val = jnp.split(u, 2, axis=-1)
        y = (jax.nn.gelu(gate) * val) @ w_down[l]
        x = x + rms_norm(y, g_post_ffn[l])
    return x


_drawn_inputs = setup_inputs


def setup_inputs(seed=0):
    import zlib

    import numpy as np

    out = dict(_drawn_inputs(seed))
    spreads = {}
    factors = {'b_gate': 8.0,
     'lambda_k1': 3.094,
     'lambda_q2': 3.257,
     'subln_gain': 4.823,
     'pool_scale': 4.654,
     'g_post_mix': 3.388,
     'g_pre_ffn': 3.308,
     'conv_b': 3.469,
     'g_post_ffn': 4.961}
    for name, (base, spread) in spreads.items():
        noise = np.random.default_rng([zlib.crc32(name.encode()), seed]).standard_normal(out[name].shape)
        drawn = base * np.exp(spread * noise) if base else spread * noise
        out[name] = __import__('jax').numpy.asarray(drawn.astype(out[name].dtype))
    for name, factor in factors.items():
        out[name] = (out[name] * factor).astype(out[name].dtype)
    return out
```

```python
from contextlib import ExitStack
import math

import numpy as np

import concourse.bass as bass
from concourse import mybir

F32 = mybir.dt.float32
F32R = mybir.dt.float32r
ACT = mybir.ActivationFunctionType
ALU = mybir.AluOpType
AX = mybir.AxisListType

P = 128
D = 2048
S = 256
TT = S // P
KC = D // P
HEADS = 8
HD = 64
AW = HEADS * 2 * HD
AC = AW // P
PW = D // 2
PC = PW // P
WINDOWS = (2, 4, 8, 16)
PAD = max(WINDOWS) // 2
PROW = S + 2 * PAD
DFF = (11 * D // 4) // P * P
FC = DFF // P
EPS = 1e-6
SUBLN_EPS = 1e-5
SCALE = HD ** -0.5
LAMBDA_INIT = 0.8 - 0.6 * math.exp(0.0)
PIECE = 2048
SLOTS = 4
GK = PIECE // S
WB = 512

Q_P = 4
Q_V = Q_P + 2
Q_GATE = Q_V + 2
Q_BRANCH = Q_GATE + 8
Q_OUT = Q_BRANCH + 4
Q_UP = Q_OUT + KC // SLOTS
Q_DOWN = Q_UP + FC // 2
Q_END = Q_DOWN + FC // SLOTS

COL = {}
_at = 0
for _name, _n in (("g_pre_mix", KC), ("g_pre_ffn", KC), ("b_gate", 2 * KC), ("pool_scale", PC),
                  ("subln_gain", 1), ("w0", 2 * FC), ("w1", 2 * FC), ("w2", 2 * FC), ("conv_b", 2 * FC)):
    COL[_name] = (_at, _n)
    _at += _n
NPAR = _at
C_ID, C_DIST, C_SLOPE = 0, P, P + TT * S
NCONST = C_SLOPE + HEADS

SEMAPHORES = (
    [f"{n}{s}" for n in ("w_loaded", "w_hi_ready", "w_lo_ready", "w_used") for s in range(SLOTS)]
    + [f"{n}{g}" for n in ("half_copied", "bank_free") for g in range(4)]
    + [f"x_loaded{i}" for i in range(4)] + [f"z_scaled{g}" for g in range(2)]
    + ["const_loaded", "par_loaded", "lam_loaded", "invcnt_loaded", "poolw_loaded", "xrow_loaded",
       "grow_loaded", "grow2_loaded", "out_stored",
       "ones_set", "pads_set", "half_set",
       "xT_turned", "xT_hi", "xT_lo", "x_squared", "x_var", "x_rstd", "diag_ready", "R_summed", "R_ready",
       "lam_prod", "lam_sum", "lam_exp", "lam_ready", "gain_scaled", "bias_halved",
       "p_ready", "window_step", "mixed_ready", "pooled", "pool_scaled", "v_ready",
       "head_qk", "head_v", "scores_done", "t_biased", "t_max", "exp_done", "sum_inv", "lam_inv",
       "p1_scaled", "probs_ready", "pT_turned", "pT_ready", "o_done", "o_squared", "o_var", "o_rstd",
       "o_scaled", "oT_turned", "oT_hi", "oT_lo", "neg_max", "gate_ready", "yp_hi", "yp_lo",
       "gated0", "gated1", "merged_ready", "first_hi", "first_lo", "y_done", "y_squared", "y_var",
       "y_rstd", "y_scaled", "x1_ready", "x1_turned", "x1T_hi", "x1T_lo", "x1_squared", "x1_var",
       "x1_rstd", "tap0", "tap1", "tap2", "gelu_ready", "act_ready", "y2_done", "y2_squared",
       "y2_var", "y2_rstd", "y2_scaled", "out_ready"])


def build(nc, x, w_in, w_attn_branch, pool_w, w_pool_branch, w_out, w_up, w_down,
          g_post_mix, g_post_ffn, lambdas, params, consts, invcnt, out):
    with ExitStack() as ctx:
        place = [(nc.sbuf_base + 31) // 32 * 32]
        spans = {}

        def sb(name, shape, dt=F32, at=None):
            size = int(np.prod(shape[1:])) * 4
            if at is None:
                at = place[0]
                place[0] += (size + 31) // 32 * 32
            assert at + size <= 229344, (name, at + size)
            spans[name] = at
            return nc.alloc_sbuf_tensor_at(name, shape, dt, offset=at)

        w_raw = [sb(f"w_raw{s}", [P, PIECE]) for s in range(SLOTS)]
        w_hi = [sb(f"w_hi{s}", [P, PIECE], F32R) for s in range(SLOTS)]
        w_lo = [sb(f"w_lo{s}", [P, PIECE], F32R) for s in range(SLOTS)]
        xT = sb("xT", [P, 2, KC, S], F32R)
        tmp = [sb(f"tmp{g}", [P, 2, S]) for g in range(2)]
        z = [sb(f"z{g}", [P, 2, S + 2]) for g in range(2)]
        cst = sb("cst", [P, NCONST])
        par = sb("par", [P, NPAR])
        ones = sb("ones", [P, P])
        R = sb("R", [P, 1, S])
        ss = sb("ss", [P, 8])
        var = sb("var", [P, 8])
        rstd = sb("rstd", [P, 8])
        half = sb("half", [P, 2])
        hbias = sb("hbias", [P, 2 * KC])
        gain = sb("gain", [P, 1])
        small = sb("small", [P, 32])
        U = place[0]
        qk = sb("qk", [P, 2, HEADS, S])
        v = sb("v", [P, TT, AW])
        ppad = sb("ppad", [P, PC, PROW])
        gates = sb("gates", [P, 2 * KC, S])
        t = [sb(f"t{u}", [P, 2, S]) for u in range(TT)]
        probs = sb("probs", [P, TT, S])
        pT = sb("pT", [P, TT, S])
        qk_head = sb("qk_head", [P, 2, S])
        v_head = sb("v_head", [P, TT, P])
        o = sb("o", [P, TT, P])
        U_end = place[0]
        oT = sb("oT", [P, 2, HEADS, S], F32R, at=spans["qk"])
        pooled = sb("pooled", [P, PC, S], at=spans["ppad"])
        xs = sb("xs", [P, TT, D], at=spans["gates"])
        junk = sb("junk", [P, D], at=spans["gates"] + 16384)
        mixed = sb("mixed", [P, PC, S], at=spans["gates"])
        win = [sb(f"win{i}", [P, 2, PROW], at=spans["gates"] + 8192 + 2176 * i) for i in range(2)]
        icnt = sb("icnt", [P, 4, 1, S], at=spans["gates"] + 16384 + 2048 * 2)
        pw = sb("pw", [P, 4, 2, S], at=spans["gates"] + 24576)
        lamv = sb("lamv", [P, 2, 2, HD], at=spans["probs"])
        lamp = sb("lamp", [P, 2, HD], at=spans["probs"] + 1024)
        yp = sb("yp", [P, 2, PC, S], F32R, at=spans["xT"])
        merged = sb("merged", [P, KC, S], at=spans["xT"] + 16384)
        place[0] = U
        chunk = sb("chunk", [P, SLOTS, 2, S], F32R)
        G = sb("G", [P, 2, S])
        grow = sb("grow", [P, D])
        xrow = sb("xrow", [P, TT, D])
        hidden = sb("hidden", [P, FC, S])
        ybuf = sb("ybuf", [P, TT, D], at=spans["hidden"])
        junk2 = sb("junk2", [P, D], at=spans["hidden"] + 16384)

        ps = ctx.enter_context(nc.psum_tensor("ps", [P, 8, WB], F32))
        sem = {n: ctx.enter_context(nc.semaphore(n)) for n in SEMAPHORES}
        w_loaded, w_hi_ready, w_lo_ready, w_used = (
            [sem[f"{n}{s}"] for s in range(SLOTS)] for n in ("w_loaded", "w_hi_ready", "w_lo_ready", "w_used"))
        half_copied, bank_free = (
            [sem[f"{n}{g}"] for g in range(4)] for n in ("half_copied", "bank_free"))
        z_scaled = [sem["z_scaled0"], sem["z_scaled1"]]
        gated = [sem["gated0"], sem["gated1"]]

        ident = cst[:, C_ID:C_ID + P]
        dist = cst[:, C_DIST:C_DIST + TT * S].rearrange("p (u o k) -> p u o k", u=TT, o=1)
        diag = tmp[1][:, 0, :]
        rmax = small[:, 0:4].rearrange("p (u c) -> p u c", u=TT)
        nmax = small[:, 4:8].rearrange("p (u c) -> p u c", u=TT)
        esum = small[:, 8:12].rearrange("p (u c) -> p u c", u=TT)
        einv = small[:, 12:16].rearrange("p (u c) -> p u c", u=TT)
        linv = small[:, 16:18]
        lsum = small[:, 18:20]
        lexp = small[:, 20:22]
        lam = small[:, 22:23]

        def column(name, n=0):
            return par[:, bass.ds(COL[name][0] + n, 1)] if not isinstance(n, int) else \
                par[:, COL[name][0] + n:COL[name][0] + n + 1]

        def zt(g):
            return z[g][:, :, 1:S + 1]

        def pair(g, half_no):
            return ps[:, 2 * g:2 * g + 2, half_no * S:(half_no + 1) * S]

        block = ctx.enter_context(nc.Block())

        @block.sync
        def _(sp):
            def columns(w, h, col):
                return w.rearrange("(h k p) n -> h p k n", p=P, k=GK)[h, :, :, bass.ds(col, S)]

            def load(slot, q, src, first=False):
                if not first:
                    sp.wait_ge(w_lo_ready[slot], q)
                n = src.shape[-1]
                sp.dma_start(w_raw[slot][:, :].rearrange("p (k n) -> p k n", n=n) if len(src.shape) == 3
                             else w_raw[slot][:, :], src).then_inc(w_loaded[slot], 16)

            x_v = x.rearrange("(u p) d -> p u d", p=P)

            def load_x(i):
                sp.dma_start(xs[:, :, WB * i:WB * (i + 1)], x_v[:, :, WB * i:WB * (i + 1)]).then_inc(sem[f"x_loaded{i}"], 16)

            load_x(0)
            load_x(1)
            load(0, 0, columns(w_in, 0, 0), first=True)
            load_x(2)
            load_x(3)
            load(1, 0, columns(w_in, 1, 0), first=True)
            load(2, 0, columns(w_in, 0, S), first=True)
            load(3, 0, columns(w_in, 1, S), first=True)

            def in_quads(first, last, col0):
                with sp.Fori(first, last) as q:
                    c0 = sp.snap((q - first) * (2 * S) + col0)
                    c1 = sp.snap((q - first) * (2 * S) + col0 + S)
                    for slot in range(SLOTS):
                        load(slot, q, columns(w_in, slot % 2, c0 if slot < 2 else c1))

            in_quads(1, Q_P, 2 * S)
            in_quads(Q_P, Q_V, 3 * AW)
            sp.wait_ge(sem["x_squared"], TT)
            sp.wait_ge(sem["xT_lo"], KC)
            sp.dma_start(icnt[:, :, :, :].rearrange("p g o s -> p (g o s)"), invcnt).then_inc(sem["invcnt_loaded"], 16)
            sp.dma_start(pw[:, :, :, :].rearrange("p g k n -> p (g k) n"),
                         pool_w.rearrange("g (k p) n -> p (g k) n", p=P)).then_inc(sem["poolw_loaded"], 16)
            for q in range(Q_V, Q_GATE):
                for slot in range(SLOTS):
                    col = 2 * AW + WB * (q - Q_V)
                    load(slot, q, w_in.rearrange("(h k p) n -> h p k n", p=P, k=4)[slot, :, :, col:col + WB])
            in_quads(Q_GATE, Q_BRANCH, 3 * AW + PW)
            with sp.Fori(Q_BRANCH, Q_OUT) as q:
                c0 = sp.snap((q - Q_BRANCH) * (2 * S))
                c1 = sp.snap((q - Q_BRANCH) * (2 * S) + S)
                for slot in range(SLOTS):
                    load(slot, q, columns(w_pool_branch if slot % 2 else w_attn_branch, 0, c0 if slot < 2 else c1))

            def row_quads(w, first, last):
                with sp.Fori(first, last) as q:
                    rows = [sp.snap((q - first) * (SLOTS * P) + P * s) for s in range(SLOTS)]
                    for slot in range(SLOTS):
                        load(slot, q, w[bass.ds(rows[slot], P), :])

            for slot in range(SLOTS):
                load(slot, Q_OUT, w_out[P * slot:P * slot + P, :])
            sp.wait_ge(sem["merged_ready"], 8)
            sp.wait_ge(w_used[3], Q_OUT)
            sp.dma_start(xrow[:, :, :], x_v).then_inc(sem["xrow_loaded"], 16)
            sp.dma_start(grow[:, :], g_post_mix.to_broadcast([P, D])).then_inc(sem["grow_loaded"], 16)
            with sp.Fori(Q_OUT + 1, Q_UP) as q:
                rows = [sp.snap((q - Q_OUT) * (SLOTS * P) + P * s) for s in range(SLOTS)]
                for slot in range(SLOTS):
                    load(slot, q, w_out[bass.ds(rows[slot], P), :])
            with sp.Fori(Q_UP, Q_DOWN) as q:
                c0 = sp.snap((q - Q_UP) * S)
                c1 = sp.snap((q - Q_UP) * S + DFF)
                for slot in range(SLOTS):
                    load(slot, q, columns(w_up, slot % 2, c0 if slot < 2 else c1))
            sp.wait_ge(sem["y_scaled"], 2 * SLOTS)
            sp.dma_start(grow[:, :], g_post_ffn.to_broadcast([P, D])).then_inc(sem["grow2_loaded"], 16)
            row_quads(w_down, Q_DOWN, Q_END)
            out_v = out.rearrange("(u p) d -> u p d", p=P)
            for u in range(TT):
                for b in range(4):
                    sp.wait_ge(sem["out_ready"], 4 * u + b + 1)
                    sp.dma_start(out_v[u, :, WB * b:WB * (b + 1)], xrow[:, u, WB * b:WB * (b + 1)]).then_inc(sem["out_stored"], 16)
            sp.wait_ge(sem["out_stored"], 16 * 4 * TT)

        @block.gpsimd
        def _(pool):
            pool.memset(half[:, :], -0.5).then_inc(sem["half_set"], 1)
            pool.memset(ppad[:, :, 0:PAD], 0.0)
            pool.memset(ppad[:, :, PAD + S:PROW], 0.0).then_inc(sem["pads_set"], 1)

            def power(var_ready, n, col, width, done):
                pool.wait_ge(sem[var_ready], n)
                nc.gpsimd.tensor_tensor(rstd[:, col:col + width], var[:, col:col + width], half[:, 0:width],
                                        ALU.pow).then_inc(sem[done], 1)

            pool.wait_ge(sem["half_set"], 1)
            power("x_var", 1, 0, 2, "x_rstd")

            steps = 0
            pool.wait_ge(sem["pads_set"], 1)
            pool.wait_ge(sem["invcnt_loaded"], 16)
            for grp, window in enumerate(WINDOWS):
                pool.wait_ge(sem["p_ready"], grp + 1)
                if grp:
                    pool.wait_ge(sem["mixed_ready"], grp)
                src = ppad[:, 2 * grp:2 * grp + 2, :]
                length, reach, at = PROW, 1, 0
                while reach < window:
                    length -= reach
                    nc.gpsimd.tensor_tensor(win[at][:, :, 0:length], src[:, :, 0:length], src[:, :, reach:reach + length],
                                            ALU.add).then_inc(sem["window_step"], 1)
                    steps += 1
                    pool.wait_ge(sem["window_step"], steps)
                    src, at, reach = win[at], 1 - at, 2 * reach
                first = PAD - window // 2
                nc.gpsimd.tensor_tensor(win[at][:, :, 0:S], src[:, :, first:first + S],
                                        icnt[:, grp, :, :].to_broadcast([P, 2, S]), ALU.mult).then_inc(sem["window_step"], 1)
                steps += 1
                pool.wait_ge(sem["window_step"], steps)
                nc.gpsimd.tensor_tensor(mixed[:, 2 * grp:2 * grp + 2, :], win[at][:, :, 0:S],
                                        ppad[:, 2 * grp:2 * grp + 2, PAD:PAD + S], ALU.subtract).then_inc(sem["mixed_ready"], 1)

            nc.gpsimd.tensor_copy(qk_head[:, :, :], qk[:, :, 0, :]).then_inc(sem["head_qk"], 1)
            pool.wait_ge(sem["v_ready"], 4)
            nc.gpsimd.tensor_copy(v_head[:, :, :], v[:, :, 0:P]).then_inc(sem["head_v"], 1)
            with pool.Fori(1, HEADS) as h:
                vcol = pool.snap(h * P)
                pool.wait_ge(sem["scores_done"], h)
                nc.gpsimd.tensor_copy(qk_head[:, :, :], qk[:, :, bass.ds(h, 1), :].rearrange("p a o s -> p a (o s)")).then_inc(sem["head_qk"], 1)
                pool.wait_ge(sem["o_var"], h)
                nc.gpsimd.tensor_tensor(rstd[:, 2:4], var[:, 2:4], half[:, 0:2], ALU.pow).then_inc(sem["o_rstd"], 1)
                nc.gpsimd.tensor_copy(v_head[:, :, :], v[:, :, bass.ds(vcol, P)]).then_inc(sem["head_v"], 1)
            power("o_var", HEADS, 2, 2, "o_rstd")
            for u in range(TT):
                power("y_var", u + 1, 4 + u, 1, "y_rstd")
            power("x1_var", 1, 0, 2, "x1_rstd")
            for u in range(TT):
                power("y2_var", u + 1, 6 + u, 1, "y2_rstd")

        @block.scalar
        def _(act):
            def split_hi(slot, q, q1, d1):
                act.wait_ge(w_loaded[slot], d1)
                if not (isinstance(q, int) and q == 0):
                    act.wait_ge(w_used[slot], q)
                nc.scalar.activation(w_hi[slot][:, :], w_raw[slot][:, :], ACT.Copy).then_inc(w_hi_ready[slot], 1)

            def copy_half(g, slot, q1):
                act.wait_ge(w_used[slot], q1)
                nc.scalar.activation(tmp[g % 2][:, :, :], pair(g, 1), ACT.Copy).then_inc(half_copied[g], 1)

            act.dma_start(cst[:, :], consts).then_inc(sem["const_loaded"], 16)
            act.dma_start(par[:, :], params).then_inc(sem["par_loaded"], 16)
            act.dma_start(lamv[:, :, :, :].rearrange("p a b d -> p (a b d)"), lambdas.to_broadcast([P, 4 * HD])).then_inc(sem["lam_loaded"], 16)

            def turn_hi(c):
                act.wait_ge(sem["xT_turned"], c // 4 + 1)
                src = ps[:, 4 + 2 * (c // 4 % 2) + c % 4 // 2, (c % 2) * S:(c % 2 + 1) * S]
                nc.scalar.activation(xT[:, 0, c, :], src, ACT.Copy, scale=column("g_pre_mix", c)).then_inc(sem["xT_hi"], 1)

            act.wait_ge(sem["par_loaded"], 16)
            for c in range(8):
                turn_hi(c)
            split_hi(0, 0, 1, 16)
            for c in range(8, KC):
                turn_hi(c)
            split_hi(1, 0, 1, 16)
            for u in range(TT):
                if u:
                    act.wait_ge(sem["x_squared"], u)
                nc.scalar.activation(junk[:, :], xs[:, u, :], ACT.Square, accum_out=ss[:, u:u + 1]).then_inc(sem["x_squared"], 1)
            split_hi(2, 0, 1, 16)
            nc.scalar.mul(hbias[:, :], par[:, COL["b_gate"][0]:COL["b_gate"][0] + 2 * KC], 0.5).then_inc(sem["bias_halved"], 1)
            nc.scalar.mul(gain[:, :], column("subln_gain"), 1.0 - LAMBDA_INIT).then_inc(sem["gain_scaled"], 1)
            act.wait_ge(sem["lam_sum"], 1)
            nc.scalar.activation(lexp, lsum, ACT.Exp).then_inc(sem["lam_exp"], 1)
            act.wait_ge(sem["R_summed"], 1)
            nc.scalar.copy(R[:, 0, :], ps[:, 7, 0:S]).then_inc(sem["R_ready"], 1)

            def splits(q, slots):
                for slot in slots:
                    split_hi(slot, q, q + 1, 16 * (q + 1))

            for q in range(Q_V):
                splits(q, [3])
                splits(q + 1, [0])
                copy_half(0, 1, q + 1)
                splits(q + 1, [1, 2])
                copy_half(1, 3, q + 1)
            for q in range(Q_V, Q_GATE):
                splits(q, [3])
                splits(q + 1, [0, 1])
                if q == Q_GATE - 1:
                    for n in range(PC):
                        act.wait_ge(sem["pooled"], n // 2 + 1)
                        ins = nc.scalar.activation(pooled[:, n, :], ps[:, 4 + n // 2, (n % 2) * S:(n % 2 + 1) * S],
                                                   ACT.Copy, scale=column("pool_scale", n))
                        if n % 4 == 3:
                            ins.then_inc(bank_free[2 + n // 4], 1)
                splits(q + 1, [2])
                act.wait_ge(w_used[3], q + 1)
                for u in range(TT):
                    nc.scalar.activation(v[:, u, WB * (q - Q_V):WB * (q - Q_V + 1)], ps[:, 2 * (q - Q_V) + u, :],
                                         ACT.Copy, scale=rstd[:, u:u + 1]).then_inc(sem["v_ready"], 1)

            act.wait_ge(sem["bias_halved"], 1)
            act.wait_ge(sem["gain_scaled"], 1)
            with act.Fori(Q_GATE, Q_BRANCH) as q:
                q1, q2, d1, d2 = act.snap(q + 1), act.snap(q + 2), act.snap(q * 16 + 16), act.snap(q * 16 + 32)
                n, h, h1, hu = act.snap(q - 3), act.snap(q - Q_GATE), act.snap(q - Q_GATE + 1), act.snap((q - Q_GATE) * 2 + 1)
                hu2 = act.snap((q - Q_GATE) * 2 + 2)
                tile = act.snap((q - Q_GATE) * 4)
                for u in range(TT):
                    act.wait_ge(sem["neg_max"], hu if u == 0 else hu2)
                    for c in range(2):
                        ins = nc.scalar.activation(t[u][:, c, :], t[u][:, c, :], ACT.Exp, bias=nmax[:, u, c:c + 1],
                                                   scale=SCALE, accum_out=esum[:, u, c:c + 1])
                    ins.then_inc(sem["exp_done"], 1)
                split_hi(3, q, q1, d1)
                split_hi(0, q1, q2, d2)

                def tanh(g):
                    act.wait_ge(z_scaled[g], n)
                    for j in range(2):
                        at = act.snap(tile + (2 * g + j))
                        ins = nc.scalar.activation(gates[:, bass.ds(at, 1), :], z[g][:, j:j + 1, 1:S + 1], ACT.Tanh,
                                                   bias=hbias[:, bass.ds(at, 1)], scale=0.5)
                    ins.then_inc(sem["gate_ready"], 1)

                copy_half(0, 1, q1)
                split_hi(1, q1, q2, d2)
                tanh(0)
                act.wait_ge(sem["o_done"], h1)
                for u in range(TT):
                    ins = nc.scalar.activation(o[:, u, :], ps[:, 7, u * P:(u + 1) * P], ACT.Square, accum_out=ss[:, 2 + u:3 + u])
                ins.then_inc(sem["o_squared"], 1)
                act.wait_ge(sem["o_rstd"], h1)
                for u in range(TT):
                    ins = nc.scalar.activation(o[:, u, :], ps[:, 7, u * P:(u + 1) * P], ACT.Copy, scale=rstd[:, 2 + u:3 + u])
                ins.then_inc(sem["o_scaled"], 1)
                split_hi(2, q1, q2, d2)
                act.wait_ge(sem["oT_turned"], h1)
                nc.scalar.activation(oT[:, 0, bass.ds(h, 1), :], ps[:, 6:7, 0:S], ACT.Copy, scale=gain[:, 0:1]).then_inc(sem["oT_hi"], 1)
                copy_half(1, 3, q1)
                tanh(1)

            nc.scalar.activation(yp[:, 0, :, :], pooled[:, :, :], ACT.Copy).then_inc(sem["yp_hi"], 1)
            with act.Fori(Q_BRANCH, Q_OUT) as q:
                q1, q2, d1, d2 = act.snap(q + 1), act.snap(q + 2), act.snap(q * 16 + 16), act.snap(q * 16 + 32)
                n, m = act.snap(q - 1), act.snap(q - Q_BRANCH + 1)
                split_hi(3, q, q1, d1)
                act.wait_ge(bank_free[2], m)
                copy_half(0, 0, q1)
                split_hi(0, q1, q2, d2)
                act.wait_ge(bank_free[3], m)
                copy_half(1, 1, q1)
                split_hi(1, q1, q2, d2)
                act.wait_ge(bank_free[0], n)
                copy_half(2, 2, q1)
                split_hi(2, q1, q2, d2)
                act.wait_ge(bank_free[1], n)
                copy_half(3, 3, q1)

            def chunk_hi(slot, src, scale):
                return nc.scalar.activation(chunk[:, slot:slot + 1, 0, :], src, ACT.Copy, scale=scale)

            def row_phase(src, scale, first, last, ready):
                act.wait_ge(*ready)
                for slot in range(3):
                    chunk_hi(slot, src[:, slot:slot + 1, :], scale).then_inc(sem["first_hi"], 1)
                with act.Fori(first, last - 1) as q:
                    q1, q2, d1, d2 = act.snap(q + 1), act.snap(q + 2), act.snap(q * 16 + 16), act.snap(q * 16 + 32)
                    k = [act.snap((q - first) * SLOTS + 3 + s) for s in range(SLOTS)]
                    for i, slot in enumerate((3, 0, 1, 2)):
                        act.wait_ge(w_used[slot], q if slot == 3 else q1)
                        chunk_hi(slot, src[:, bass.ds(k[i], 1), :], scale)
                        if slot == 3:
                            split_hi(3, q, q1, d1)
                        else:
                            split_hi(slot, q1, q2, d2)
                act.wait_ge(w_used[3], last - 1)
                chunk_hi(3, src[:, SLOTS * (last - first) - 1:SLOTS * (last - first), :], scale)
                splits(last - 1, [3])

            row_phase(merged, 0.5, Q_OUT, Q_UP, (sem["merged_ready"], 8))

            def square(src, col, done, out_to):
                nc.scalar.activation(out_to, src, ACT.Square, accum_out=ss[:, col:col + 1]).then_inc(sem[done], 1)

            def y_rows(u):
                return ps[:, 4 * u:4 * u + 4, :].rearrange("p b n -> p (b n)")

            act.wait_ge(sem["y_done"], 1)
            square(y_rows(0), 4, "y_squared", junk2[:, :])
            splits(Q_UP, [0, 1, 2])
            act.wait_ge(w_used[3], Q_UP)
            act.wait_ge(sem["y_squared"], 1)
            square(y_rows(1), 5, "y_squared", junk2[:, :])

            def x1T_hi(u, c):
                act.wait_ge(sem["x1_turned"], 4 * u + c // 4 + 1)
                nc.scalar.activation(xT[:, 0, c, u * P:(u + 1) * P], ps[:, 4 * u + c // 4, (c % 4) * P:(c % 4 + 1) * P], ACT.Copy,
                                     scale=column("g_pre_ffn", c)).then_inc(sem["x1T_hi"], 1)

            for u in range(TT):
                for c in range(KC):
                    x1T_hi(u, c)
            for u in range(TT):
                act.wait_ge(sem["y_squared"], 2)
                if u:
                    act.wait_ge(sem["x1_squared"], u)
                square(xrow[:, u, :], u, "x1_squared", junk2[:, :])
            act.wait_ge(sem["R_summed"], 2)
            nc.scalar.copy(R[:, 0, :], ps[:, 7, 0:S]).then_inc(sem["R_ready"], 1)

            with act.Fori(Q_UP, Q_DOWN) as q:
                q1, q2, d1, d2 = act.snap(q + 1), act.snap(q + 2), act.snap(q * 16 + 16), act.snap(q * 16 + 32)
                n = act.snap(q - 11)

                def taps(g):
                    act.wait_ge(z_scaled[g], n)
                    for j in range(2):
                        ft = act.snap((q - Q_UP) * 2 + (FC * g + j))
                        ins = nc.scalar.activation(tmp[g][:, j, :], z[g][:, j, 1:S + 1], ACT.Identity,
                                                   bias=column("conv_b", ft), scale=column("w1", ft))
                    ins.then_inc(sem[f"tap{g}"], 1)

                split_hi(3, q, q1, d1)
                split_hi(0, q1, q2, d2)
                copy_half(0, 1, q1)
                split_hi(1, q1, q2, d2)
                taps(0)
                split_hi(2, q1, q2, d2)
                act.wait_ge(sem["gated0"], act.snap((q - Q_UP) * 4 + (4 + GATED0)))
                nc.scalar.activation(G[:, :, :], tmp[0][:, :, :], ACT.Gelu_apprx_tanh).then_inc(sem["gelu_ready"], 1)
                copy_half(1, 3, q1)
                taps(1)

            row_phase(hidden, 1.0, Q_DOWN, Q_END, (sem["act_ready"], Q_DOWN - Q_UP))
            act.wait_ge(sem["y2_done"], 1)
            square(y_rows(0), 6, "y2_squared", junk2[:, :])
            act.wait_ge(w_used[3], Q_END)
            act.wait_ge(sem["y2_squared"], 1)
            square(y_rows(1), 7, "y2_squared", junk2[:, :])

        @block.vector
        def _(dve):
            def split_lo(slot, q1):
                dve.wait_ge(w_hi_ready[slot], q1)
                nc.vector.tensor_tensor(w_lo[slot][:, :], w_raw[slot][:, :], w_hi[slot][:, :].bitcast(F32),
                                        ALU.subtract).then_inc(w_lo_ready[slot], 1)

            def sum_halves(g, n):
                dve.wait_ge(half_copied[g], n)
                nc.vector.tensor_tensor(zt(g % 2), pair(g, 0), tmp[g % 2][:, :, :], ALU.add).then_inc(bank_free[g], 1)

            def scale_tokens(g, n, dst):
                dve.wait_ge(bank_free[g], n)
                return nc.vector.tensor_tensor(dst, zt(g), R[:, :, :].to_broadcast([P, 2, S]), ALU.mult)

            nc.vector.memset(ones[:, :], 1.0).then_inc(sem["ones_set"], 1)
            for g in range(2):
                nc.vector.memset(z[g][:, :, :], 0.0).then_inc(sem["ones_set"], 1)

            def turn_lo(c):
                dve.wait_ge(sem["xT_hi"], c - c % 2 + 2)
                src = ps[:, 4 + 2 * (c // 4 % 2) + c % 4 // 2, (c % 2) * S:(c % 2 + 1) * S]
                nc.vector.scalar_tensor_tensor(xT[:, 1, c, :], src, column("g_pre_mix", c), xT[:, 0, c, :].bitcast(F32),
                                               ALU.mult, ALU.subtract).then_inc(sem["xT_lo"], 1)

            for c in range(8):
                turn_lo(c)
            split_lo(0, 1)
            for c in range(8, KC):
                turn_lo(c)
            split_lo(1, 1)

            def variance(squared, n, col, width, size, eps, done):
                dve.wait_ge(sem[squared], n)
                nc.vector.tensor_scalar(var[:, col:col + width], ss[:, col:col + width], 1.0 / size, eps,
                                        ALU.mult, ALU.add).then_inc(sem[done], 1)

            def diagonal(rstd_ready):
                dve.wait_ge(sem[rstd_ready], 1)
                for u in range(TT):
                    ins = nc.vector.tensor_scalar(diag[:, u * P:(u + 1) * P], ident, rstd[:, u:u + 1], None, ALU.mult)
                ins.then_inc(sem["diag_ready"], 1)

            variance("x_squared", TT, 0, 2, D, EPS, "x_var")
            split_lo(2, 1)
            diagonal("x_rstd")
            dve.wait_ge(sem["lam_loaded"], 16)
            nc.vector.tensor_tensor(lamp[:, :, :], lamv[:, :, 0, :], lamv[:, :, 1, :], ALU.mult).then_inc(sem["lam_prod"], 1)
            dve.wait_ge(sem["lam_prod"], 1)
            nc.vector.tensor_reduce(lsum, lamp[:, :, :], AX.X, ALU.add).then_inc(sem["lam_sum"], 1)
            dve.wait_ge(sem["lam_exp"], 1)
            nc.vector.scalar_tensor_tensor(lam, lexp[:, 0:1], LAMBDA_INIT, lexp[:, 1:2], ALU.add, ALU.subtract).then_inc(sem["lam_ready"], 1)
            dve.wait_ge(sem["R_ready"], 1)
            dve.wait_ge(sem["ones_set"], 3)

            for q in range(Q_V):
                split_lo(3, q + 1)
                split_lo(0, q + 2)
                for g in range(2):
                    if g:
                        split_lo(1, q + 2)
                        split_lo(2, q + 2)
                    sum_halves(g, q + 1)
                    if q < Q_P:
                        tile = 4 * (q % 2) + 2 * g
                        scale_tokens(g, q + 1, qk[:, q // 2, tile:tile + 2, :]).then_inc(z_scaled[g], 1)
                    else:
                        tile = 4 * (q - Q_P) + 2 * g
                        scale_tokens(g, q + 1, ppad[:, tile:tile + 2, PAD:PAD + S]).then_inc(sem["p_ready"], 1)
            for q in range(Q_V, Q_GATE):
                split_lo(3, q + 1)
                for slot in range(3):
                    split_lo(slot, q + 2)

            dve.wait_ge(sem["lam_ready"], 1)
            with dve.Fori(Q_GATE, Q_BRANCH) as q:
                q1, q2, n, h, h1 = dve.snap(q + 1), dve.snap(q + 2), dve.snap(q - 1), dve.snap(q - Q_GATE), dve.snap(q - Q_GATE + 1)
                hu = [dve.snap((q - Q_GATE) * 2 + (1 + u)) for u in range(TT)]
                dve.wait_ge(sem["scores_done"], h1)
                for u in range(TT):
                    nc.vector.scalar_tensor_tensor(t[u][:, :, :], dist[:, u, :, :].to_broadcast([P, 2, S]),
                                                   cst[:, bass.ds(dve.snap(h + C_SLOPE), 1)], ps[:, 4:6, u * S:(u + 1) * S],
                                                   ALU.mult, ALU.add).then_inc(sem["t_biased"], 1)
                    dve.wait_ge(sem["t_biased"], hu[u])
                    nc.vector.tensor_reduce(rmax[:, u, :], t[u][:, :, :], AX.X, ALU.max).then_inc(sem["t_max"], 1)
                    dve.wait_ge(sem["t_max"], hu[u])
                    nc.vector.tensor_scalar(nmax[:, u, :], rmax[:, u, :], -SCALE, None, ALU.mult).then_inc(sem["neg_max"], 1)
                split_lo(3, q1)
                for u in range(TT):
                    dve.wait_ge(sem["exp_done"], hu[u])
                    nc.vector.reciprocal(einv[:, u, :], esum[:, u, :]).then_inc(sem["sum_inv"], 1)
                    dve.wait_ge(sem["sum_inv"], hu[u])
                    nc.vector.tensor_scalar(linv[:, u:u + 1], einv[:, u, 1:2], lam, None, ALU.mult).then_inc(sem["lam_inv"], 1)
                    dve.wait_ge(sem["lam_inv"], hu[u])
                    nc.vector.tensor_scalar(t[u][:, 1, :], t[u][:, 1, :], linv[:, u:u + 1], None, ALU.mult).then_inc(sem["p1_scaled"], 1)
                    dve.wait_ge(sem["p1_scaled"], hu[u])
                    nc.vector.scalar_tensor_tensor(probs[:, u, :], t[u][:, 0, :], einv[:, u, 0:1], t[u][:, 1, :],
                                                   ALU.mult, ALU.subtract).then_inc(sem["probs_ready"], 1)
                split_lo(0, q2)
                dve.wait_ge(sem["pT_turned"], h1)
                nc.vector.tensor_copy(pT[:, :, :], ps[:, 6, :].rearrange("p (k s) -> p k s", k=TT)).then_inc(sem["pT_ready"], 1)
                sum_halves(0, n)
                scale_tokens(0, n, zt(0)).then_inc(z_scaled[0], 1)
                split_lo(1, q2)
                dve.wait_ge(sem["o_squared"], h1)
                nc.vector.tensor_scalar(var[:, 2:4], ss[:, 2:4], 1.0 / P, SUBLN_EPS, ALU.mult, ALU.add).then_inc(sem["o_var"], 1)
                split_lo(2, q2)
                dve.wait_ge(sem["oT_hi"], h1)
                nc.vector.scalar_tensor_tensor(oT[:, 1, bass.ds(h, 1), :], ps[:, 6:7, 0:S], gain[:, 0:1],
                                               oT[:, 0, bass.ds(h, 1), :].bitcast(F32), ALU.mult, ALU.subtract).then_inc(sem["oT_lo"], 1)
                sum_halves(1, n)
                scale_tokens(1, n, zt(1)).then_inc(z_scaled[1], 1)

            dve.wait_ge(sem["yp_hi"], 1)
            nc.vector.tensor_tensor(yp[:, 1, :, :], pooled[:, :, :], yp[:, 0, :, :].bitcast(F32), ALU.subtract).then_inc(sem["yp_lo"], 1)
            dve.wait_ge(sem["gate_ready"], 16)
            with dve.Fori(Q_BRANCH, Q_OUT) as q:
                q1, q2, n, m = dve.snap(q + 1), dve.snap(q + 2), dve.snap(q - 1), dve.snap(q - Q_BRANCH + 1)
                m1 = dve.snap(q - Q_BRANCH + 2)
                a1 = [dve.snap((q - Q_BRANCH) * 2 + (1 + s)) for s in range(2)]

                def gate(g, count, tile, done):
                    dve.wait_ge(bank_free[g], count)
                    nc.vector.scalar_tensor_tensor(zt(g % 2), gates[:, bass.ds(tile, 2), :], 1.0, zt(g % 2),
                                                   ALU.add, ALU.mult).then_inc(sem[f"gated{g % 2}"], 1)
                    dve.wait_ge(sem[f"gated{g % 2}"], done)

                for s in range(2):
                    split_lo(3 if s == 0 else 1, q1 if s == 0 else q2)
                    tile = dve.snap((q - Q_BRANCH) * 4 + 2 * s)
                    tile2 = dve.snap((q - Q_BRANCH) * 4 + (2 * s + KC))
                    sum_halves(2 * s, n if s == 0 else m)
                    gate(2 * s, n if s == 0 else m1, tile, a1[s])
                    split_lo(2 * s, q2)
                    sum_halves(2 * s + 1, n if s == 0 else m)
                    gate(2 * s + 1, n if s == 0 else m1, tile2, a1[s])
                    nc.vector.tensor_tensor(merged[:, bass.ds(tile, 2), :], zt(0), zt(1), ALU.add).then_inc(sem["merged_ready"], 1)
                    dve.wait_ge(sem["merged_ready"], a1[s])

            def chunk_lo(slot, src, scale):
                return nc.vector.scalar_tensor_tensor(chunk[:, slot:slot + 1, 1, :], src, scale, chunk[:, slot:slot + 1, 0, :].bitcast(F32),
                                                      ALU.mult, ALU.subtract)

            def row_phase(src, scale, first, last, done):
                for slot in range(3):
                    dve.wait_ge(sem["first_hi"], done + slot + 1)
                    chunk_lo(slot, src[:, slot:slot + 1, :], scale).then_inc(sem["first_lo"], 1)
                with dve.Fori(first, last - 1) as q:
                    q1, q2 = dve.snap(q + 1), dve.snap(q + 2)
                    k = [dve.snap((q - first) * SLOTS + 3 + s) for s in range(SLOTS)]
                    for i, slot in enumerate((3, 0, 1, 2)):
                        dve.wait_ge(w_hi_ready[slot], q1 if slot == 3 else q2)
                        chunk_lo(slot, src[:, bass.ds(k[i], 1), :], scale)
                        split_lo(slot, q1 if slot == 3 else q2)
                dve.wait_ge(w_hi_ready[3], last)
                chunk_lo(3, src[:, SLOTS * (last - first) - 1:SLOTS * (last - first), :], scale)
                split_lo(3, last)

            dve.wait_ge(sem["merged_ready"], 8)
            row_phase(merged, 0.5, Q_OUT, Q_UP, 0)

            def post_norm(u, b, rstd_col, scaled, count, done):
                nc.vector.scalar_tensor_tensor(ybuf[:, u, WB * b:WB * (b + 1)], ps[:, 4 * u + b, :], rstd[:, rstd_col:rstd_col + 1],
                                               grow[:, WB * b:WB * (b + 1)], ALU.mult, ALU.mult).then_inc(sem[scaled], 1)
                dve.wait_ge(sem[scaled], count)
                nc.vector.tensor_tensor(xrow[:, u, WB * b:WB * (b + 1)], ybuf[:, u, WB * b:WB * (b + 1)],
                                        xrow[:, u, WB * b:WB * (b + 1)], ALU.add).then_inc(sem[done], 1)

            def x1T_lo(u, c):
                dve.wait_ge(sem["x1T_hi"], KC * u + c - c % 4 + 4)
                nc.vector.scalar_tensor_tensor(xT[:, 1, c, u * P:(u + 1) * P], ps[:, 4 * u + c // 4, (c % 4) * P:(c % 4 + 1) * P],
                                               column("g_pre_ffn", c), xT[:, 0, c, u * P:(u + 1) * P].bitcast(F32),
                                               ALU.mult, ALU.subtract).then_inc(sem["x1T_lo"], 1)

            dve.wait_ge(sem["xrow_loaded"], 16)
            dve.wait_ge(sem["grow_loaded"], 16)
            for u in range(TT):
                variance("y_squared", u + 1, 4 + u, 1, D, EPS, "y_var")
                if u:
                    for c in range(KC // 2):
                        x1T_lo(0, c)
                dve.wait_ge(sem["y_rstd"], u + 1)
                for b in range(4):
                    post_norm(u, b, 4 + u, "y_scaled", 4 * u + b + 1, "x1_ready")
                if u == 0:
                    for slot in range(3):
                        split_lo(slot, Q_UP + 1)
            for c in range(KC // 2, KC):
                x1T_lo(0, c)
            for c in range(KC):
                x1T_lo(1, c)
            variance("x1_squared", TT, 0, 2, D, EPS, "x1_var")
            dve.wait_ge(sem["x1_rstd"], 1)
            for u in range(TT):
                ins = nc.vector.tensor_scalar(diag[:, u * P:(u + 1) * P], ident, rstd[:, u:u + 1], None, ALU.mult)
            ins.then_inc(sem["diag_ready"], 1)
            dve.wait_ge(sem["R_ready"], 2)

            with dve.Fori(Q_UP, Q_DOWN) as q:
                q1, q2, n, i1 = dve.snap(q + 1), dve.snap(q + 2), dve.snap(q - 5), dve.snap(q - Q_UP + 1)
                def conv(g):
                    dve.wait_ge(sem[f"tap{g}"], i1)
                    for j in range(2):
                        ft = dve.snap((q - Q_UP) * 2 + (FC * g + j))
                        done = sem[f"gated{g}"]
                        nc.vector.scalar_tensor_tensor(tmp[g][:, j, :], z[g][:, j, 0:S], column("w0", ft), tmp[g][:, j, :],
                                                       ALU.mult, ALU.add).then_inc(done, 1)
                        dve.wait_ge(done, dve.snap((q - Q_UP) * 4 + (2 * j + 1 + GATED0)))
                        nc.vector.scalar_tensor_tensor(tmp[g][:, j, :], z[g][:, j, 2:S + 2], column("w2", ft), tmp[g][:, j, :],
                                                       ALU.mult, ALU.add).then_inc(done, 1)

                split_lo(3, q1)
                split_lo(0, q2)
                sum_halves(0, n)
                scale_tokens(0, n, zt(0)).then_inc(z_scaled[0], 1)
                split_lo(1, q2)
                conv(0)
                split_lo(2, q2)
                sum_halves(1, n)
                scale_tokens(1, n, zt(1)).then_inc(z_scaled[1], 1)
                conv(1)
                dve.wait_ge(sem["gated1"], dve.snap((q - Q_UP) * 4 + (4 + GATED0)))
                dve.wait_ge(sem["gelu_ready"], i1)
                tile = dve.snap((q - Q_UP) * 2)
                nc.vector.tensor_tensor(hidden[:, bass.ds(tile, 2), :], G[:, :, :], tmp[1][:, :, :], ALU.mult).then_inc(sem["act_ready"], 1)

            dve.wait_ge(sem["act_ready"], Q_DOWN - Q_UP)
            row_phase(hidden, 1.0, Q_DOWN, Q_END, 3)
            dve.wait_ge(sem["grow2_loaded"], 16)
            for u in range(TT):
                variance("y2_squared", u + 1, 6 + u, 1, D, EPS, "y2_var")
                dve.wait_ge(sem["y2_rstd"], u + 1)
                for b in range(4):
                    post_norm(u, b, 6 + u, "y2_scaled", 4 * u + b + 1, "out_ready")

        @block.tensor
        def _(pe):
            def ready(slot, q1):
                pe.wait_ge(w_hi_ready[slot], q1)
                pe.wait_ge(w_lo_ready[slot], q1)

            def column_piece(slot, q1, g, moving, c0, last, first=True):
                ready(slot, q1)
                for k in range(GK):
                    c = c0 + k
                    if moving is None:
                        pe.wait_ge(*chunk_wait(c))
                    for j in range(2):
                        col = slice(k * S + j * P, k * S + (j + 1) * P)
                        mv = moving or xT
                        nc.tensor.matmul(ps[:, 2 * g + j, :].rearrange("p (a s) -> p a s", a=2), w_hi[slot][:, col], mv[:, :, c, :],
                                         start=(k == 0 and first), stop=False, skip_group_check=True)
                        ins = nc.tensor.matmul(ps[:, 2 * g + j, 0:S], w_lo[slot][:, col], mv[:, 0, c, :],
                                               start=False, stop=(k == GK - 1 and last), skip_group_check=True)
                ins.then_inc(w_used[slot], 1)

            def token_piece(slot, u, moving_of, stationary_of, bank_of, groups, first, last):
                for w, hl in ((w_hi, 0), (w_lo, 0), (w_hi, 1)):
                    for g in range(groups):
                        ins = nc.tensor.matmul(ps[:, bank_of(g), :], stationary_of(hl), moving_of(w, g),
                                               start=(first and w is w_hi and hl == 0), stop=(last and hl == 1),
                                               skip_group_check=True)
                return ins

            def turn_x(i):
                pe.wait_ge(sem[f"x_loaded{i}"], 16)
                if i >= 2:
                    pe.wait_ge(sem["xT_lo"], 4 * (i - 1))
                for k in range(4):
                    for u in range(TT):
                        ins = nc.tensor.transpose(ps[:, 4 + 2 * (i % 2) + k // 2, (k % 2) * S + u * P:(k % 2) * S + (u + 1) * P],
                                                  xs[:, u, (4 * i + k) * P:(4 * i + k + 1) * P], ident)
                ins.then_inc(sem["xT_turned"], 1)

            def spread_R():
                nc.tensor.matmul(ps[:, 7, 0:S], ones[:, :], diag, start=True, stop=True).then_inc(sem["R_summed"], 1)

            pe.wait_ge(sem["const_loaded"], 16)
            turn_x(0)
            turn_x(1)
            pe.wait_ge(sem["xT_lo"], 8)
            column_piece(0, 1, 0, xT, 0, False)
            turn_x(2)
            turn_x(3)
            pe.wait_ge(sem["xT_lo"], KC)
            column_piece(1, 1, 0, xT, GK, True, first=False)
            column_piece(2, 1, 1, xT, 0, False)
            pe.wait_ge(sem["diag_ready"], 1)
            spread_R()
            column_piece(3, 1, 1, xT, GK, True, first=False)
            with pe.Fori(1, Q_V) as q:
                q1 = pe.snap(q + 1)
                for g in range(2):
                    pe.wait_ge(bank_free[g], q)
                    column_piece(2 * g, q1, g, xT, 0, False)
                    column_piece(2 * g + 1, q1, g, xT, GK, True, first=False)

            for q in range(Q_V, Q_GATE):
                pe.wait_ge(bank_free[q - Q_V], Q_V)
                for slot in range(SLOTS):
                    if q == Q_GATE - 1 and slot == 2:
                        pe.wait_ge(sem["poolw_loaded"], 16)
                        for grp in range(4):
                            pe.wait_ge(sem["mixed_ready"], grp + 1)
                            for j in range(2):
                                for k in range(2):
                                    ins = nc.tensor.matmul(ps[:, 4 + grp, j * S:(j + 1) * S], pw[:, grp, k, j * P:(j + 1) * P],
                                                           mixed[:, 2 * grp + k, :], start=(k == 0), stop=(k == 1), skip_group_check=True)
                            ins.then_inc(sem["pooled"], 1)
                    ready(slot, q + 1)
                    for k in range(4):
                        c = 4 * slot + k
                        for u in range(TT):
                            ins = token_piece(slot, u, lambda w, g: w[slot][:, WB * k:WB * (k + 1)],
                                              lambda hl: xT[:, hl, c, u * P:(u + 1) * P],
                                              lambda g: 2 * (q - Q_V) + u, 1, c == 0, c == KC - 1)
                    ins.then_inc(w_used[slot], 1)

            pe.wait_ge(sem["v_ready"], 4)
            pe.wait_ge(bank_free[2], 1)
            pe.wait_ge(bank_free[3], 1)
            with pe.Fori(Q_GATE, Q_BRANCH) as q:
                q1, nf, h1 = pe.snap(q + 1), pe.snap(q - 2), pe.snap(q - Q_GATE + 1)
                hu2 = pe.snap((q - Q_GATE) * 2 + 2)
                pe.wait_ge(sem["head_qk"], h1)
                for c in range(2):
                    rows = slice(c * HD, (c + 1) * HD)
                    for u in range(TT):
                        ins = nc.tensor.matmul(ps[:, 4 + c, u * S:(u + 1) * S], qk_head[rows, 0, u * P:(u + 1) * P],
                                               qk_head[rows, 1, :], start=True, stop=True, skip_group_check=True)
                ins.then_inc(sem["scores_done"], 1)
                pe.wait_ge(bank_free[0], nf)
                column_piece(0, q1, 0, xT, 0, False)
                column_piece(1, q1, 0, xT, GK, True, first=False)
                pe.wait_ge(sem["probs_ready"], hu2)
                for u in range(TT):
                    for k in range(TT):
                        ins = nc.tensor.transpose(ps[:, 6, k * S + u * P:k * S + (u + 1) * P], probs[:, u, k * P:(k + 1) * P], ident)
                ins.then_inc(sem["pT_turned"], 1)
                pe.wait_ge(bank_free[1], nf)
                column_piece(2, q1, 1, xT, 0, False)
                pe.wait_ge(sem["pT_ready"], h1)
                pe.wait_ge(sem["head_v"], h1)
                for u in range(TT):
                    for k in range(TT):
                        ins = nc.tensor.matmul(ps[:, 7, u * P:(u + 1) * P], pT[:, k, u * P:(u + 1) * P], v_head[:, k, :],
                                               start=(k == 0), stop=(k == TT - 1), skip_group_check=True)
                ins.then_inc(sem["o_done"], 1)
                column_piece(3, q1, 1, xT, GK, True, first=False)
                pe.wait_ge(sem["o_scaled"], h1)
                for u in range(TT):
                    ins = nc.tensor.transpose(ps[:, 6, u * P:(u + 1) * P], o[:, u, :], ident)
                ins.then_inc(sem["oT_turned"], 1)

            with pe.Fori(Q_BRANCH, Q_OUT) as q:
                q1, nf, mf = pe.snap(q + 1), pe.snap(q - 2), pe.snap(q - Q_BRANCH + 1)
                for g in range(4):
                    if g % 2:
                        pe.wait_ge(sem["yp_lo"], 1)
                    else:
                        pe.wait_ge(sem["oT_lo"], HEADS)
                    pe.wait_ge(bank_free[g], nf if g < 2 else mf)
                    column_piece(g, q1, g, yp if g % 2 else oT, 0, True)

            def row_piece(slot, u, first, last):
                return token_piece(slot, u, lambda w, g: w[slot][:, WB * g:WB * (g + 1)],
                                   lambda hl: chunk[:, slot, hl, u * P:(u + 1) * P],
                                   lambda g: 4 * u + g, 4, first, last)

            def row_phase(first, last, done, between=None):
                def quad(q1, is_first):
                    for slot in range(SLOTS):
                        ready(slot, q1)
                        for u in range(TT):
                            ins = row_piece(slot, u, is_first and slot == 0, False)
                        ins.then_inc(w_used[slot], 1)

                quad(first + 1, True)
                with pe.Fori(first + 1, last - 1) as q:
                    quad(pe.snap(q + 1), False)
                for u in range(TT):
                    for slot in range(SLOTS):
                        if u == 0:
                            ready(slot, last)
                        if between and u == 1 and slot == 3:
                            between()
                        ins = row_piece(slot, u, False, slot == 3)
                        if u == 1:
                            ins.then_inc(w_used[slot], 1)
                    if u == 0:
                        ins.then_inc(done, 1)

            def turn_x1(u, b):
                pe.wait_ge(sem["x1_ready"], 4 * u + b + 1)
                for k in range(4):
                    c = 4 * b + k
                    ins = nc.tensor.transpose(ps[:, 4 * u + b, k * P:(k + 1) * P], xrow[:, u, c * P:(c + 1) * P], ident)
                ins.then_inc(sem["x1_turned"], 1)

            pe.wait_ge(bank_free[2], 5)
            pe.wait_ge(bank_free[3], 5)
            pe.wait_ge(bank_free[0], 18 - 0)
            pe.wait_ge(bank_free[1], 18)
            pe.wait_ge(sem["first_hi"], 3)
            pe.wait_ge(sem["first_lo"], 3)
            row_phase(Q_OUT, Q_UP, sem["y_done"], between=lambda: [turn_x1(0, b) for b in range(2)])
            for b in range(2, 4):
                turn_x1(0, b)
            for b in range(4):
                turn_x1(1, b)

            def chunk_wait(c):
                return sem["x1T_lo"], KC + c + 1

            column_piece(0, Q_UP + 1, 0, None, 0, False)
            column_piece(1, Q_UP + 1, 0, None, GK, True, first=False)
            column_piece(2, Q_UP + 1, 1, xT, 0, False)
            pe.wait_ge(sem["diag_ready"], 2)
            spread_R()
            column_piece(3, Q_UP + 1, 1, xT, GK, True, first=False)
            with pe.Fori(Q_UP + 1, Q_DOWN) as q:
                q1, nf = pe.snap(q + 1), pe.snap(q - 6)
                for g in range(2):
                    pe.wait_ge(bank_free[g], nf)
                    column_piece(2 * g, q1, g, xT, 0, False)
                    column_piece(2 * g + 1, q1, g, xT, GK, True, first=False)

            for g in range(2):
                pe.wait_ge(bank_free[g], Q_DOWN - 6)
            pe.wait_ge(sem["first_hi"], 6)
            pe.wait_ge(sem["first_lo"], 6)
            row_phase(Q_DOWN, Q_END, sem["y2_done"])


GATED0 = 8


def kernel(**inputs):
    import numpy as np
    import concourse.bacc as bacc
    from concourse.bass_utils import run_bass_kernel_spmd

    def feature_columns(a):
        return np.ascontiguousarray(a.reshape(-1, P).T)

    g = {k: np.asarray(a) for k, a in inputs.items()}
    conv = g["conv_w"][0]
    params = np.concatenate([feature_columns(a) for a in (
        g["g_pre_mix"][0], g["g_pre_ffn"][0], g["b_gate"][0], g["pool_scale"][0], g["subln_gain"][0],
        conv[0], conv[1], conv[2], g["conv_b"][0])], axis=1)
    lambdas = np.concatenate([g["lambda_q1"], g["lambda_k1"], g["lambda_q2"], g["lambda_k2"]], axis=1)

    keys = np.arange(S)
    dist = np.abs(np.arange(P)[:, None, None] + P * np.arange(TT)[None, :, None] - keys[None, None, :])
    slopes = np.array([-(2.0 ** (-8.0 * (h + 1) / HEADS)) / SCALE for h in range(HEADS)])
    consts = np.concatenate([np.eye(P), dist.reshape(P, TT * S), np.tile(slopes, (P, 1))], axis=1).astype(np.float32)
    counts = np.stack([np.minimum(keys + w // 2, S) - np.maximum(keys - w // 2, 0) for w in WINDOWS])
    invcnt = np.ascontiguousarray(np.broadcast_to((1.0 / counts).reshape(1, -1), (P, 4 * S)).astype(np.float32))

    arrays = {"x": g["x"][0], "w_in": g["w_in"][0], "w_attn_branch": g["w_attn_branch"][0], "pool_w": g["pool_w"][0],
              "w_pool_branch": g["w_pool_branch"][0], "w_out": g["w_out"][0], "w_up": g["w_up"][0], "w_down": g["w_down"][0],
              "g_post_mix": g["g_post_mix"], "g_post_ffn": g["g_post_ffn"], "lambdas": lambdas, "params": params,
              "consts": consts, "invcnt": invcnt}
    arrays = {k: np.ascontiguousarray(a) for k, a in arrays.items()}
    nc = bacc.Bacc("TRN2", target_bir_lowering=False, num_devices=1, dynamic_dma_scratch_size=1024)
    args = [nc.dram_tensor(f"in_{k}", a.shape, F32, kind="ExternalInput").ap() for k, a in arrays.items()]
    out = nc.dram_tensor("out", (S, D), F32, kind="ExternalOutput").ap()
    build(nc, *args, out)
    r = run_bass_kernel_spmd(nc, [{f"in_{k}": a for k, a in arrays.items()}], core_ids=[0])
    return r.results[0]["out"].reshape(1, S, D)
```

```python
from contextlib import ExitStack
import math

import numpy as np

import concourse.bass as bass
from concourse import mybir

F32 = mybir.dt.float32
F32R = mybir.dt.float32r
ACT = mybir.ActivationFunctionType
ALU = mybir.AluOpType
AX = mybir.AxisListType

P = 128
D = 2048
S = 256
TT = S // P
KC = D // P
HEADS = 8
HD = 64
AW = HEADS * 2 * HD
AC = AW // P
PW = D // 2
PC = PW // P
WINDOWS = (2, 4, 8, 16)
PAD = max(WINDOWS) // 2
PROW = S + 2 * PAD
DFF = (11 * D // 4) // P * P
FC = DFF // P
EPS = 1e-6
SUBLN_EPS = 1e-5
SCALE = HD ** -0.5
LAMBDA_INIT = 0.8 - 0.6 * math.exp(0.0)
PIECE = 2048
SLOTS = 4
GK = PIECE // S
WB = 512

Q_P = 4
Q_V = Q_P + 2
Q_GATE = Q_V + 2
Q_BRANCH = Q_GATE + 8
Q_OUT = Q_BRANCH + 4
Q_UP = Q_OUT + KC // SLOTS
Q_DOWN = Q_UP + FC // 2
Q_END = Q_DOWN + FC // SLOTS

COL = {}
_at = 0
for _name, _n in (("g_pre_mix", KC), ("b_gate", 2 * KC), ("pool_scale", PC),
                  ("subln_gain", 1), ("w0", 2 * FC), ("w1", 2 * FC), ("w2", 2 * FC), ("conv_b", 2 * FC)):
    COL[_name] = (_at, _n)
    _at += _n
NPAR = _at
C_ID, C_DIST, C_SLOPE = 0, P, P + TT * S
NCONST = C_SLOPE + HEADS

SEMAPHORES = (
    [f"{n}{s}" for n in ("w_loaded", "w_hi_ready", "w_lo_ready", "w_used") for s in range(SLOTS)]
    + [f"{n}{g}" for n in ("half_copied", "bank_free") for g in range(4)]
    + [f"x_loaded{i}" for i in range(4)] + [f"z_scaled{g}" for g in range(2)]
    + ["const_loaded", "par_loaded", "lam_loaded", "invcnt_loaded", "poolw_loaded", "xrow_loaded",
       "grow_loaded", "g2row_loaded", "grow2_loaded", "first_loaded", "first_w_hi", "first_w_lo", "out_stored",
       "ones_set", "pads_set", "half_set",
       "xT_turned", "xT_hi", "xT_lo", "x_squared", "x_var", "x_rstd", "diag_ready", "R_summed", "R_ready",
       "lam_prod", "lam_sum", "lam_exp", "lam_ready", "gain_scaled", "bias_halved",
       "p_ready", "window_step", "mixed_ready", "pooled", "pool_scaled", "v_ready",
       "head_qk", "head_v", "scores_done", "t_biased", "t_max", "exp_done", "sum_inv", "lam_inv",
       "p1_scaled", "probs_ready", "pT_turned", "pT_ready", "o_done", "o_squared", "o_var", "o_rstd",
       "o_scaled", "oT_turned", "oT_hi", "oT_lo", "neg_max", "gate_ready", "yp_hi", "yp_lo",
       "gated0", "gated1", "merged_ready", "first_hi", "first_lo", "y_done", "y_squared", "y_var",
       "y_rstd", "y_scaled", "x1_ready", "x1_turned", "x1T_hi", "x1T_lo", "x1g_ready0", "x1g_ready1", "x1g_first", "y_summed", "x1_squared", "x1_var",
       "x1_rstd", "tap0", "tap1", "tap2", "gelu_ready", "x1_pool", "out_pool", "act_ready", "y2_done", "y2_squared",
       "y2_summed", "y2_var", "y2_rstd", "y2_scaled", "out_ready"])


def build(nc, x, w_in, w_attn_branch, pool_w, w_pool_branch, w_out, w_up, w_down,
          g_post_mix, g_pre_ffn, g_post_ffn, lambdas, params, consts, invcnt, out):
    with ExitStack() as ctx:
        place = [(nc.sbuf_base + 31) // 32 * 32]
        spans = {}

        def sb(name, shape, dt=F32, at=None):
            size = int(np.prod(shape[1:])) * 4
            if at is None:
                at = place[0]
                place[0] += (size + 31) // 32 * 32
            assert at + size <= 229344, (name, at + size)
            spans[name] = at
            return nc.alloc_sbuf_tensor_at(name, shape, dt, offset=at)

        w_raw = [sb(f"w_raw{s}", [P, PIECE]) for s in range(SLOTS)]
        w_hi = [sb(f"w_hi{s}", [P, PIECE], F32R) for s in range(SLOTS)]
        w_lo = [sb(f"w_lo{s}", [P, PIECE], F32R) for s in range(SLOTS)]
        xT = sb("xT", [P, 2, KC, S], F32R)
        tmp = [sb(f"tmp{g}", [P, 2, S]) for g in range(2)]
        z = [sb(f"z{g}", [P, 2, S + 2]) for g in range(2)]
        cst = sb("cst", [P, NCONST])
        par = sb("par", [P, NPAR])
        ones = sb("ones", [P, P])
        R = sb("R", [P, 1, S])
        ss = sb("ss", [P, 20])
        ysum = sb("ysum", [P, 4])
        var = sb("var", [P, 8])
        rstd = sb("rstd", [P, 8])
        half = sb("half", [P, 2])
        hbias = sb("hbias", [P, 2 * KC])
        gain = sb("gain", [P, 1])
        small = sb("small", [P, 32])
        U = place[0]
        qk = sb("qk", [P, 2, HEADS, S])
        v = sb("v", [P, TT, AW])
        ppad = sb("ppad", [P, PC, PROW])
        gates = sb("gates", [P, 2 * KC, S])
        t = [sb(f"t{u}", [P, 2, S]) for u in range(TT)]
        probs = sb("probs", [P, TT, S])
        pT = sb("pT", [P, TT, S])
        qk_head = sb("qk_head", [P, 2, S])
        v_head = sb("v_head", [P, TT, P])
        o = sb("o", [P, TT, P])
        U_end = place[0]
        oT = sb("oT", [P, 2, HEADS, S], F32R, at=spans["qk"])
        pooled = sb("pooled", [P, PC, S], at=spans["ppad"])
        xs = sb("xs", [P, TT, D], at=spans["gates"])
        junk = sb("junk", [P, D], at=spans["gates"] + 16384)
        mixed = sb("mixed", [P, PC, S], at=spans["gates"])
        win = [sb(f"win{i}", [P, 2, PROW], at=spans["gates"] + 8192 + 2176 * i) for i in range(2)]
        icnt = sb("icnt", [P, 4, 1, S], at=spans["gates"] + 16384 + 2048 * 2)
        pw = sb("pw", [P, 4, 2, S], at=spans["gates"] + 24576)
        lamv = sb("lamv", [P, 2, 2, HD], at=spans["probs"])
        lamp = sb("lamp", [P, 2, HD], at=spans["probs"] + 1024)
        yp = sb("yp", [P, 2, PC, S], F32R, at=spans["xT"])
        merged = sb("merged", [P, KC, S], at=spans["xT"] + 16384)
        place[0] = U
        chunk = sb("chunk", [P, SLOTS, 2, S], F32R)
        G = sb("G", [P, 2, S])
        grow = sb("grow", [P, D])
        xrow = sb("xrow", [P, TT, D])
        hidden = sb("hidden", [P, FC, S])
        ybuf = sb("ybuf", [P, TT, D], at=spans["hidden"])
        junk2 = sb("junk2", [P, D], at=spans["hidden"] + 16384)
        g2row = sb("g2row", [P, D], at=spans["hidden"] + 24576)

        ps = ctx.enter_context(nc.psum_tensor("ps", [P, 8, WB], F32))
        sem = {n: ctx.enter_context(nc.semaphore(n)) for n in SEMAPHORES}
        w_loaded, w_hi_ready, w_lo_ready, w_used = (
            [sem[f"{n}{s}"] for s in range(SLOTS)] for n in ("w_loaded", "w_hi_ready", "w_lo_ready", "w_used"))
        half_copied, bank_free = (
            [sem[f"{n}{g}"] for g in range(4)] for n in ("half_copied", "bank_free"))
        z_scaled = [sem["z_scaled0"], sem["z_scaled1"]]
        gated = [sem["gated0"], sem["gated1"]]

        ident = cst[:, C_ID:C_ID + P]
        dist = cst[:, C_DIST:C_DIST + TT * S].rearrange("p (u o k) -> p u o k", u=TT, o=1)
        diag = tmp[1][:, 0, :]
        rmax = small[:, 0:4].rearrange("p (u c) -> p u c", u=TT)
        nmax = small[:, 4:8].rearrange("p (u c) -> p u c", u=TT)
        esum = small[:, 8:12].rearrange("p (u c) -> p u c", u=TT)
        einv = small[:, 12:16].rearrange("p (u c) -> p u c", u=TT)
        linv = small[:, 16:18]
        lsum = small[:, 18:20]
        lexp = small[:, 20:22]
        lam = small[:, 22:23]

        def column(name, n=0):
            return par[:, bass.ds(COL[name][0] + n, 1)] if not isinstance(n, int) else \
                par[:, COL[name][0] + n:COL[name][0] + n + 1]

        def zt(g):
            return z[g][:, :, 1:S + 1]

        def turn_bank(c):
            return (4, 5, 6, 7, 2, 3, 4, 5)[c // 2]

        def pair(g, half_no):
            return ps[:, 2 * g:2 * g + 2, half_no * S:(half_no + 1) * S]

        def value(eng, n):
            return n if isinstance(n, int) else eng.snap(n)

        def quad_values(eng, q):
            return value(eng, q + 1), value(eng, q + 2), value(eng, q * 16 + 16), value(eng, q * 16 + 32)

        block = ctx.enter_context(nc.Block())

        @block.sync
        def _(sp):
            def columns(w, h, col):
                return w.rearrange("(h k p) n -> h p k n", p=P, k=GK)[h, :, :, bass.ds(col, S)]

            def load(slot, q, src, first=False):
                if not first:
                    sp.wait_ge(w_lo_ready[slot], q)
                n = src.shape[-1]
                sp.dma_start(w_raw[slot][:, :].rearrange("p (k n) -> p k n", n=n) if len(src.shape) == 3
                             else w_raw[slot][:, :], src).then_inc(w_loaded[slot], 16)

            x_v = x.rearrange("(u p) d -> p u d", p=P)

            def load_x(i):
                sp.dma_start(xs[:, :, WB * i:WB * (i + 1)], x_v[:, :, WB * i:WB * (i + 1)]).then_inc(sem[f"x_loaded{i}"], 16)

            load_x(0)
            first_half = w_raw[0][:, :].rearrange("p (a k n) -> p a k n", a=2, n=S)
            first_src = columns(w_in, 0, 0).rearrange("p (a k) n -> p a k n", a=2)
            sp.dma_start(first_half[:, 0, :, :], first_src[:, 0, :, :]).then_inc(sem["first_loaded"], 16)
            load_x(1)
            sp.dma_start(first_half[:, 1, :, :], first_src[:, 1, :, :]).then_inc(w_loaded[0], 16)
            load_x(2)
            load_x(3)
            load(1, 0, columns(w_in, 1, 0), first=True)
            load(2, 0, columns(w_in, 0, S), first=True)
            load(3, 0, columns(w_in, 1, S), first=True)

            def in_quads(first, last, col0):
                with sp.Fori(first, last) as q:
                    c0 = sp.snap((q - first) * (2 * S) + col0)
                    c1 = sp.snap((q - first) * (2 * S) + col0 + S)
                    for slot in range(SLOTS):
                        load(slot, q, columns(w_in, slot % 2, c0 if slot < 2 else c1))

            in_quads(1, Q_P, 2 * S)
            in_quads(Q_P, Q_V, 3 * AW)
            sp.wait_ge(sem["x_squared"], TT)
            sp.wait_ge(sem["xT_lo"], KC)
            sp.dma_start(icnt[:, :, :, :].rearrange("p g o s -> p (g o s)"), invcnt).then_inc(sem["invcnt_loaded"], 16)
            sp.dma_start(pw[:, :, :, :].rearrange("p g k n -> p (g k) n"),
                         pool_w.rearrange("g (k p) n -> p (g k) n", p=P)).then_inc(sem["poolw_loaded"], 16)
            for q in range(Q_V, Q_GATE):
                for slot in range(SLOTS):
                    col = 2 * AW + WB * (q - Q_V)
                    load(slot, q, w_in.rearrange("(h k p) n -> h p k n", p=P, k=4)[slot, :, :, col:col + WB])
            in_quads(Q_GATE, Q_BRANCH, 3 * AW + PW)
            with sp.Fori(Q_BRANCH, Q_OUT) as q:
                c0 = sp.snap((q - Q_BRANCH) * (2 * S))
                c1 = sp.snap((q - Q_BRANCH) * (2 * S) + S)
                for slot in range(SLOTS):
                    load(slot, q, columns(w_pool_branch if slot % 2 else w_attn_branch, 0, c0 if slot < 2 else c1))

            for q in range(Q_OUT, Q_UP):
                if q == Q_OUT + 2:
                    sp.wait_ge(sem["merged_ready"], 8)
                    sp.wait_ge(w_used[3], Q_OUT)
                    sp.dma_start(xrow[:, :, :], x_v).then_inc(sem["xrow_loaded"], 16)
                if q == Q_OUT + 3:
                    sp.dma_start(grow[:, :], g_post_mix.to_broadcast([P, D])).then_inc(sem["grow_loaded"], 16)
                    sp.dma_start(g2row[:, :], g_pre_ffn.to_broadcast([P, D])).then_inc(sem["g2row_loaded"], 16)
                for slot in range(SLOTS):
                    row = P * ((q - Q_OUT) * SLOTS + slot)
                    load(slot, q, w_out[row:row + P, :])
            with sp.Fori(Q_UP, Q_DOWN) as q:
                c0 = sp.snap((q - Q_UP) * S)
                c1 = sp.snap((q - Q_UP) * S + DFF)
                for slot in range(SLOTS):
                    load(slot, q, columns(w_up, slot % 2, c0 if slot < 2 else c1))
            sp.wait_ge(sem["y_scaled"], 2 * SLOTS)
            sp.dma_start(grow[:, :], g_post_ffn.to_broadcast([P, D])).then_inc(sem["grow2_loaded"], 16)
            with sp.Fori(Q_DOWN, Q_END) as q:
                rows = [sp.snap((q - Q_DOWN) * (SLOTS * P) + P * s) for s in range(SLOTS)]
                for slot in range(SLOTS):
                    load(slot, q, w_down[bass.ds(rows[slot], P), :])
            out_v = out.rearrange("(u p) d -> u p d", p=P)
            for u in range(TT):
                for b in range(4):
                    if b < 3:
                        sp.wait_ge(sem["out_ready"], 3 * u + b + 1)
                    else:
                        sp.wait_ge(sem["out_pool"], u + 1)
                    sp.dma_start(out_v[u, :, WB * b:WB * (b + 1)], xrow[:, u, WB * b:WB * (b + 1)]).then_inc(sem["out_stored"], 16)
            sp.wait_ge(sem["out_stored"], 16 * 4 * TT)

        @block.gpsimd
        def _(pool):
            pool.memset(half[:, :], -0.5).then_inc(sem["half_set"], 1)
            pool.memset(ppad[:, :, 0:PAD], 0.0)
            pool.memset(ppad[:, :, PAD + S:PROW], 0.0).then_inc(sem["pads_set"], 1)

            def power(var_ready, n, col, width, done):
                pool.wait_ge(sem[var_ready], n)
                nc.gpsimd.tensor_tensor(rstd[:, col:col + width], var[:, col:col + width], half[:, 0:width],
                                        ALU.pow).then_inc(sem[done], 1)

            pool.wait_ge(sem["half_set"], 1)
            power("x_var", 1, 0, 2, "x_rstd")

            steps = 0
            pool.wait_ge(sem["pads_set"], 1)
            pool.wait_ge(sem["invcnt_loaded"], 16)
            for grp, window in enumerate(WINDOWS):
                pool.wait_ge(sem["p_ready"], grp + 1)
                if grp:
                    pool.wait_ge(sem["mixed_ready"], grp)
                src = ppad[:, 2 * grp:2 * grp + 2, :]
                length, reach, at = PROW, 1, 0
                while reach < window:
                    length -= reach
                    nc.gpsimd.tensor_tensor(win[at][:, :, 0:length], src[:, :, 0:length], src[:, :, reach:reach + length],
                                            ALU.add).then_inc(sem["window_step"], 1)
                    steps += 1
                    pool.wait_ge(sem["window_step"], steps)
                    src, at, reach = win[at], 1 - at, 2 * reach
                first = PAD - window // 2
                nc.gpsimd.tensor_tensor(win[at][:, :, 0:S], src[:, :, first:first + S],
                                        icnt[:, grp, :, :].to_broadcast([P, 2, S]), ALU.mult).then_inc(sem["window_step"], 1)
                steps += 1
                pool.wait_ge(sem["window_step"], steps)
                nc.gpsimd.tensor_tensor(mixed[:, 2 * grp:2 * grp + 2, :], win[at][:, :, 0:S],
                                        ppad[:, 2 * grp:2 * grp + 2, PAD:PAD + S], ALU.subtract).then_inc(sem["mixed_ready"], 1)

            nc.gpsimd.tensor_copy(qk_head[:, :, :], qk[:, :, 0, :]).then_inc(sem["head_qk"], 1)
            pool.wait_ge(sem["v_ready"], 4)
            nc.gpsimd.tensor_copy(v_head[:, :, :], v[:, :, 0:P]).then_inc(sem["head_v"], 1)
            with pool.Fori(1, HEADS) as h:
                vcol = pool.snap(h * P)
                pool.wait_ge(sem["scores_done"], h)
                nc.gpsimd.tensor_copy(qk_head[:, :, :], qk[:, :, bass.ds(h, 1), :].rearrange("p a o s -> p a (o s)")).then_inc(sem["head_qk"], 1)
                pool.wait_ge(sem["o_var"], h)
                nc.gpsimd.tensor_tensor(rstd[:, 2:4], var[:, 2:4], half[:, 0:2], ALU.pow).then_inc(sem["o_rstd"], 1)
                nc.gpsimd.tensor_copy(v_head[:, :, :], v[:, :, bass.ds(vcol, P)]).then_inc(sem["head_v"], 1)
            power("o_var", HEADS, 2, 2, "o_rstd")

            def add_x(u, b, count):
                pool.wait_ge(sem["y_scaled"], count)
                cols = slice(WB * b, WB * (b + 1))
                nc.gpsimd.tensor_tensor(xrow[:, u, cols], ybuf[:, u, cols], xrow[:, u, cols], ALU.add).then_inc(sem["x1_pool"], 1)

            def gain_x1(u, b, name, count):
                pool.wait_ge(sem[name], count)
                cols = slice(WB * b, WB * (b + 1))
                nc.gpsimd.tensor_tensor(ybuf[:, u, cols], xrow[:, u, cols], g2row[:, cols], ALU.mult).then_inc(sem[f"x1g_ready{u}"], 1)

            power("y_var", 1, 4, 1, "y_rstd")
            pool.wait_ge(sem["g2row_loaded"], 16)
            for b in range(2):
                gain_x1(0, b, "x1_ready", b + 1)
            for b in range(2, 4):
                add_x(0, b, b + 1)
                gain_x1(0, b, "x1_pool", b - 1)
            power("y_var", 2, 5, 1, "y_rstd")
            for b in range(1, 4):
                gain_x1(1, b, "x1_ready", 2 + b + 1)
            power("x1_var", 1, 0, 2, "x1_rstd")
            for u in range(TT):
                power("y2_var", u + 1, 6 + u, 1, "y2_rstd")
                b = 3
                pool.wait_ge(sem["y2_scaled"], 4 * u + 1)
                nc.gpsimd.tensor_tensor(xrow[:, u, WB * b:WB * (b + 1)], ybuf[:, u, WB * b:WB * (b + 1)],
                                        xrow[:, u, WB * b:WB * (b + 1)], ALU.add).then_inc(sem["out_pool"], 1)

        @block.scalar
        def _(act):
            def split_hi(slot, q, q1, d1):
                act.wait_ge(w_loaded[slot], d1)
                if not (isinstance(q, int) and q == 0):
                    act.wait_ge(w_used[slot], q)
                nc.scalar.activation(w_hi[slot][:, :], w_raw[slot][:, :], ACT.Copy).then_inc(w_hi_ready[slot], 1)

            def copy_half(g, slot, q1):
                act.wait_ge(w_used[slot], q1)
                nc.scalar.activation(tmp[g % 2][:, :, :], pair(g, 1), ACT.Copy).then_inc(half_copied[g], 1)

            act.dma_start(cst[:, :], consts).then_inc(sem["const_loaded"], 16)
            act.dma_start(par[:, :], params).then_inc(sem["par_loaded"], 16)
            act.dma_start(lamv[:, :, :, :].rearrange("p a b d -> p (a b d)"), lambdas.to_broadcast([P, 4 * HD])).then_inc(sem["lam_loaded"], 16)

            def turn_hi(c):
                act.wait_ge(sem["xT_turned"], c // 4 + 1)
                src = ps[:, turn_bank(c), (c % 2) * S:(c % 2 + 1) * S]
                nc.scalar.activation(xT[:, 0, c, :], src, ACT.Copy, scale=column("g_pre_mix", c)).then_inc(sem["xT_hi"], 1)

            act.wait_ge(sem["par_loaded"], 16)
            nc.scalar.mul(hbias[:, :], par[:, COL["b_gate"][0]:COL["b_gate"][0] + 2 * KC], 0.5).then_inc(sem["bias_halved"], 1)
            nc.scalar.mul(gain[:, :], column("subln_gain"), 1.0 - LAMBDA_INIT).then_inc(sem["gain_scaled"], 1)
            H = PIECE // 2
            for c in range(4):
                turn_hi(c)
            act.wait_ge(sem["first_loaded"], 16)
            nc.scalar.activation(w_hi[0][:, 0:H], w_raw[0][:, 0:H], ACT.Copy).then_inc(sem["first_w_hi"], 1)
            for c in range(4, 8):
                turn_hi(c)
            act.wait_ge(w_loaded[0], 16)
            nc.scalar.activation(w_hi[0][:, H:], w_raw[0][:, H:], ACT.Copy).then_inc(w_hi_ready[0], 1)
            for c in range(8, KC):
                turn_hi(c)

            def square_x(u):
                if u:
                    act.wait_ge(sem["x_squared"], u)
                nc.scalar.activation(junk[:, :], xs[:, u, :], ACT.Square, accum_out=ss[:, u:u + 1]).then_inc(sem["x_squared"], 1)

            split_hi(1, 0, 1, 16)
            square_x(0)
            split_hi(2, 0, 1, 16)
            square_x(1)
            act.wait_ge(sem["lam_sum"], 1)
            nc.scalar.activation(lexp, lsum, ACT.Exp).then_inc(sem["lam_exp"], 1)

            def copy_R(n):
                act.wait_ge(sem["R_summed"], n)
                nc.scalar.copy(R[:, 0, :], ps[:, 7, 0:S]).then_inc(sem["R_ready"], 1)

            def splits(q, slots):
                for slot in slots:
                    split_hi(slot, q, q + 1, 16 * (q + 1))

            for q in range(Q_V):
                splits(q, [3])
                splits(q + 1, [0])
                if q == 0:
                    copy_R(1)
                copy_half(0, 1, q + 1)
                splits(q + 1, [1, 2])
                copy_half(1, 3, q + 1)
            for q in range(Q_V, Q_GATE):
                splits(q, [3])
                splits(q + 1, [0, 1])
                if q == Q_GATE - 1:
                    for n in range(PC):
                        act.wait_ge(sem["pooled"], n // 2 + 1)
                        ins = nc.scalar.activation(pooled[:, n, :], ps[:, 4 + n // 2, (n % 2) * S:(n % 2 + 1) * S],
                                                   ACT.Copy, scale=column("pool_scale", n))
                        if n % 4 == 3:
                            ins.then_inc(bank_free[2 + n // 4], 1)
                splits(q + 1, [2])
                act.wait_ge(w_used[3], q + 1)
                for u in range(TT):
                    nc.scalar.activation(v[:, u, WB * (q - Q_V):WB * (q - Q_V + 1)], ps[:, 2 * (q - Q_V) + u, :],
                                         ACT.Copy, scale=rstd[:, u:u + 1]).then_inc(sem["v_ready"], 1)

            act.wait_ge(sem["bias_halved"], 1)
            act.wait_ge(sem["gain_scaled"], 1)
            with act.Fori(Q_GATE, Q_BRANCH) as q:
                q1, q2, d1, d2 = act.snap(q + 1), act.snap(q + 2), act.snap(q * 16 + 16), act.snap(q * 16 + 32)
                n, h, h1, hu = act.snap(q - 3), act.snap(q - Q_GATE), act.snap(q - Q_GATE + 1), act.snap((q - Q_GATE) * 2 + 1)
                hu2 = act.snap((q - Q_GATE) * 2 + 2)
                tile = act.snap((q - Q_GATE) * 4)
                for u in range(TT):
                    act.wait_ge(sem["neg_max"], hu if u == 0 else hu2)
                    for c in range(2):
                        ins = nc.scalar.activation(t[u][:, c, :], t[u][:, c, :], ACT.Exp, bias=nmax[:, u, c:c + 1],
                                                   scale=SCALE, accum_out=esum[:, u, c:c + 1])
                    ins.then_inc(sem["exp_done"], 1)
                split_hi(3, q, q1, d1)
                split_hi(0, q1, q2, d2)

                def tanh(g):
                    act.wait_ge(z_scaled[g], n)
                    for j in range(2):
                        at = act.snap(tile + (2 * g + j))
                        ins = nc.scalar.activation(gates[:, bass.ds(at, 1), :], z[g][:, j:j + 1, 1:S + 1], ACT.Tanh,
                                                   bias=hbias[:, bass.ds(at, 1)], scale=0.5)
                    ins.then_inc(sem["gate_ready"], 1)

                copy_half(0, 1, q1)
                split_hi(1, q1, q2, d2)
                tanh(0)
                act.wait_ge(sem["o_done"], h1)
                for u in range(TT):
                    ins = nc.scalar.activation(o[:, u, :], ps[:, 7, u * P:(u + 1) * P], ACT.Square, accum_out=ss[:, 2 + u:3 + u])
                ins.then_inc(sem["o_squared"], 1)
                act.wait_ge(sem["o_rstd"], h1)
                for u in range(TT):
                    ins = nc.scalar.activation(o[:, u, :], ps[:, 7, u * P:(u + 1) * P], ACT.Copy, scale=rstd[:, 2 + u:3 + u])
                ins.then_inc(sem["o_scaled"], 1)
                split_hi(2, q1, q2, d2)
                act.wait_ge(sem["oT_turned"], h1)
                nc.scalar.activation(oT[:, 0, bass.ds(h, 1), :], ps[:, 6:7, 0:S], ACT.Copy, scale=gain[:, 0:1]).then_inc(sem["oT_hi"], 1)
                copy_half(1, 3, q1)
                tanh(1)

            for c in (slice(0, PC // 2), slice(PC // 2, PC)):
                nc.scalar.activation(yp[:, 0, c, :], pooled[:, c, :], ACT.Copy).then_inc(sem["yp_hi"], 1)
            def branch_quad(q, before_last=None):
                q1, q2, d1, d2 = quad_values(act, q)
                n, m = value(act, q - 1), value(act, q - Q_BRANCH + 1)
                split_hi(3, q, q1, d1)
                act.wait_ge(bank_free[2], m)
                copy_half(0, 0, q1)
                split_hi(0, q1, q2, d2)
                act.wait_ge(bank_free[3], m)
                copy_half(1, 1, q1)
                split_hi(1, q1, q2, d2)
                act.wait_ge(bank_free[0], n)
                copy_half(2, 2, q1)
                split_hi(2, q1, q2, d2)
                if before_last:
                    before_last()
                act.wait_ge(bank_free[1], n)
                copy_half(3, 3, q1)

            def chunk_hi(slot, src, scale):
                return nc.scalar.activation(chunk[:, slot:slot + 1, 0, :], src, ACT.Copy, scale=scale)

            def first_chunks(src, scale):
                for slot in range(3):
                    chunk_hi(slot, src[:, slot:slot + 1, :], scale).then_inc(sem["first_hi"], 1)

            def row_phase(src, scale, first, last, ready):
                act.wait_ge(*ready)
                with act.Fori(first, last - 1) as q:
                    q1, q2, d1, d2 = act.snap(q + 1), act.snap(q + 2), act.snap(q * 16 + 16), act.snap(q * 16 + 32)
                    k = [act.snap((q - first) * SLOTS + 3 + s) for s in range(SLOTS)]
                    for i, slot in enumerate((3, 0, 1, 2)):
                        act.wait_ge(w_used[slot], q if slot == 3 else q1)
                        chunk_hi(slot, src[:, bass.ds(k[i], 1), :], scale)
                        if slot == 3:
                            split_hi(3, q, q1, d1)
                        else:
                            split_hi(slot, q1, q2, d2)
                act.wait_ge(w_used[3], last - 1)
                chunk_hi(3, src[:, SLOTS * (last - first) - 1:SLOTS * (last - first), :], scale)
                splits(last - 1, [3])

            with act.Fori(Q_BRANCH, Q_OUT - 1) as q:
                branch_quad(q)
            branch_quad(Q_OUT - 1, before_last=lambda: first_chunks(merged, 0.5))
            row_phase(merged, 0.5, Q_OUT, Q_UP, (sem["merged_ready"], 8))

            def square(src, col, done, out_to):
                nc.scalar.activation(out_to, src, ACT.Square, accum_out=ss[:, col:col + 1]).then_inc(sem[done], 1)

            def square_y(u, b, col, name, last):
                if 4 * u + b < 7:
                    act.wait_ge(sem[f"{name}_done"], 4 * u + b + 1)
                else:
                    act.wait_ge(w_used[3], last)
                square(ps[:, 4 * u + b, :], col + 4 * u + b, f"{name}_squared", junk2[:, (4 * u + b) % 4 * WB:((4 * u + b) % 4 + 1) * WB])

            def x1T_hi(u, b):
                act.wait_ge(sem["x1_turned"], 4 * u + b + 1)
                nc.scalar.activation(xT[:, 0, 4 * b:4 * b + 4, u * P:(u + 1) * P], ps[:, 4 * u + b, :].rearrange("p (k s) -> p k s", k=4),
                                     ACT.Copy).then_inc(sem["x1T_hi"], 1)

            for b in range(4):
                square_y(0, b, 4, "y", Q_UP)
            splits(Q_UP, [0, 1])
            x1T_hi(0, 0)
            act.wait_ge(sem["y_squared"], 4)
            for b in range(4):
                square_y(1, b, 4, "y", Q_UP)
            for b in range(1, 4):
                x1T_hi(0, b)
            act.wait_ge(sem["y_squared"], 8)
            act.wait_ge(sem["x1_pool"], 2)
            square(xrow[:, 0, :], 0, "x1_squared", junk2[:, :])
            for b in range(4):
                x1T_hi(1, b)
            act.wait_ge(sem["x1_squared"], 1)
            square(xrow[:, 1, :], 1, "x1_squared", junk2[:, :])
            splits(Q_UP, [2])

            def up_quad(q, is_first=False, before_last=None):
                q1, q2, d1, d2 = quad_values(act, q)
                n, g4 = value(act, q - 11), value(act, (q - Q_UP) * 4 + (4 + GATED0))

                def taps(g):
                    act.wait_ge(z_scaled[g], n)
                    for j in range(2):
                        ft = value(act, (q - Q_UP) * 2 + (FC * g + j))
                        ins = nc.scalar.activation(tmp[g][:, j, :], z[g][:, j, 1:S + 1], ACT.Identity,
                                                   bias=column("conv_b", ft), scale=column("w1", ft))
                    ins.then_inc(sem[f"tap{g}"], 1)

                split_hi(3, q, q1, d1)
                split_hi(0, q1, q2, d2)
                if is_first:
                    copy_R(2)
                copy_half(0, 1, q1)
                split_hi(1, q1, q2, d2)
                taps(0)
                split_hi(2, q1, q2, d2)
                act.wait_ge(sem["gated0"], g4)
                nc.scalar.activation(G[:, :, :], tmp[0][:, :, :], ACT.Gelu_apprx_tanh).then_inc(sem["gelu_ready"], 1)
                if before_last:
                    before_last()
                copy_half(1, 3, q1)
                taps(1)

            up_quad(Q_UP, is_first=True)
            with act.Fori(Q_UP + 1, Q_DOWN - 1) as q:
                up_quad(q)
            up_quad(Q_DOWN - 1, before_last=lambda: first_chunks(hidden, 1.0))
            row_phase(hidden, 1.0, Q_DOWN, Q_END, (sem["act_ready"], Q_DOWN - Q_UP))
            for u in range(TT):
                if u:
                    act.wait_ge(sem["y2_squared"], 4)
                for b in range(4):
                    square_y(u, b, 12, "y2", Q_END)

        @block.vector
        def _(dve):
            def split_lo(slot, q1):
                dve.wait_ge(w_hi_ready[slot], q1)
                nc.vector.tensor_tensor(w_lo[slot][:, :], w_raw[slot][:, :], w_hi[slot][:, :].bitcast(F32),
                                        ALU.subtract).then_inc(w_lo_ready[slot], 1)

            def sum_halves(g, n):
                dve.wait_ge(half_copied[g], n)
                nc.vector.tensor_tensor(zt(g % 2), pair(g, 0), tmp[g % 2][:, :, :], ALU.add).then_inc(bank_free[g], 1)

            def scale_tokens(g, n, dst):
                dve.wait_ge(bank_free[g], n)
                return nc.vector.tensor_tensor(dst, zt(g), R[:, :, :].to_broadcast([P, 2, S]), ALU.mult)

            nc.vector.memset(ones[:, :], 1.0).then_inc(sem["ones_set"], 1)
            for g in range(2):
                nc.vector.memset(z[g][:, :, :], 0.0).then_inc(sem["ones_set"], 1)

            def turn_lo(c):
                dve.wait_ge(sem["xT_hi"], c - c % 2 + 2)
                src = ps[:, turn_bank(c), (c % 2) * S:(c % 2 + 1) * S]
                nc.vector.scalar_tensor_tensor(xT[:, 1, c, :], src, column("g_pre_mix", c), xT[:, 0, c, :].bitcast(F32),
                                               ALU.mult, ALU.subtract).then_inc(sem["xT_lo"], 1)

            H = PIECE // 2
            for c in range(4):
                turn_lo(c)
            dve.wait_ge(sem["first_w_hi"], 1)
            nc.vector.tensor_tensor(w_lo[0][:, 0:H], w_raw[0][:, 0:H], w_hi[0][:, 0:H].bitcast(F32), ALU.subtract).then_inc(sem["first_w_lo"], 1)
            for c in range(4, 8):
                turn_lo(c)
            dve.wait_ge(w_hi_ready[0], 1)
            nc.vector.tensor_tensor(w_lo[0][:, H:], w_raw[0][:, H:], w_hi[0][:, H:].bitcast(F32), ALU.subtract).then_inc(w_lo_ready[0], 1)
            for c in range(8, KC):
                turn_lo(c)
            split_lo(1, 1)

            def variance(squared, n, col, width, size, eps, done):
                dve.wait_ge(sem[squared], n)
                nc.vector.tensor_scalar(var[:, col:col + width], ss[:, col:col + width], 1.0 / size, eps,
                                        ALU.mult, ALU.add).then_inc(sem[done], 1)

            def diagonal(rstd_ready):
                dve.wait_ge(sem[rstd_ready], 1)
                for u in range(TT):
                    ins = nc.vector.tensor_scalar(diag[:, u * P:(u + 1) * P], ident, rstd[:, u:u + 1], None, ALU.mult)
                ins.then_inc(sem["diag_ready"], 1)

            split_lo(2, 1)
            variance("x_squared", TT, 0, 2, D, EPS, "x_var")
            dve.wait_ge(sem["ones_set"], 3)
            diagonal("x_rstd")
            dve.wait_ge(sem["lam_loaded"], 16)
            nc.vector.tensor_tensor(lamp[:, :, :], lamv[:, :, 0, :], lamv[:, :, 1, :], ALU.mult).then_inc(sem["lam_prod"], 1)
            dve.wait_ge(sem["lam_prod"], 1)
            nc.vector.tensor_reduce(lsum, lamp[:, :, :], AX.X, ALU.add).then_inc(sem["lam_sum"], 1)

            for q in range(Q_V):
                split_lo(3, q + 1)
                split_lo(0, q + 2)
                for g in range(2):
                    if g:
                        split_lo(1, q + 2)
                        split_lo(2, q + 2)
                    sum_halves(g, q + 1)
                    if q == 0:
                        dve.wait_ge(sem["R_ready"], 1)
                    if q < Q_P:
                        tile = 4 * (q % 2) + 2 * g
                        scale_tokens(g, q + 1, qk[:, q // 2, tile:tile + 2, :]).then_inc(z_scaled[g], 1)
                    else:
                        tile = 4 * (q - Q_P) + 2 * g
                        scale_tokens(g, q + 1, ppad[:, tile:tile + 2, PAD:PAD + S]).then_inc(sem["p_ready"], 1)
                if q == 0:
                    dve.wait_ge(sem["lam_exp"], 1)
                    nc.vector.scalar_tensor_tensor(lam, lexp[:, 0:1], LAMBDA_INIT, lexp[:, 1:2], ALU.add, ALU.subtract).then_inc(sem["lam_ready"], 1)
            for q in range(Q_V, Q_GATE):
                split_lo(3, q + 1)
                for slot in range(3):
                    split_lo(slot, q + 2)

            dve.wait_ge(sem["lam_ready"], 1)
            with dve.Fori(Q_GATE, Q_BRANCH) as q:
                q1, q2, n, h, h1 = dve.snap(q + 1), dve.snap(q + 2), dve.snap(q - 1), dve.snap(q - Q_GATE), dve.snap(q - Q_GATE + 1)
                hu = [dve.snap((q - Q_GATE) * 2 + (1 + u)) for u in range(TT)]
                dve.wait_ge(sem["scores_done"], h1)
                for u in range(TT):
                    nc.vector.scalar_tensor_tensor(t[u][:, :, :], dist[:, u, :, :].to_broadcast([P, 2, S]),
                                                   cst[:, bass.ds(dve.snap(h + C_SLOPE), 1)], ps[:, 4:6, u * S:(u + 1) * S],
                                                   ALU.mult, ALU.add).then_inc(sem["t_biased"], 1)
                    dve.wait_ge(sem["t_biased"], hu[u])
                    nc.vector.tensor_reduce(rmax[:, u, :], t[u][:, :, :], AX.X, ALU.max).then_inc(sem["t_max"], 1)
                    dve.wait_ge(sem["t_max"], hu[u])
                    nc.vector.tensor_scalar(nmax[:, u, :], rmax[:, u, :], -SCALE, None, ALU.mult).then_inc(sem["neg_max"], 1)
                for u in range(TT):
                    dve.wait_ge(sem["exp_done"], hu[u])
                    nc.vector.reciprocal(einv[:, u, :], esum[:, u, :]).then_inc(sem["sum_inv"], 1)
                    dve.wait_ge(sem["sum_inv"], hu[u])
                    nc.vector.tensor_scalar(linv[:, u:u + 1], einv[:, u, 1:2], lam, None, ALU.mult).then_inc(sem["lam_inv"], 1)
                    dve.wait_ge(sem["lam_inv"], hu[u])
                    nc.vector.tensor_scalar(t[u][:, 1, :], t[u][:, 1, :], linv[:, u:u + 1], None, ALU.mult).then_inc(sem["p1_scaled"], 1)
                    dve.wait_ge(sem["p1_scaled"], hu[u])
                    nc.vector.scalar_tensor_tensor(probs[:, u, :], t[u][:, 0, :], einv[:, u, 0:1], t[u][:, 1, :],
                                                   ALU.mult, ALU.subtract).then_inc(sem["probs_ready"], 1)
                split_lo(3, q1)
                split_lo(0, q2)
                dve.wait_ge(sem["pT_turned"], h1)
                nc.vector.tensor_copy(pT[:, :, :], ps[:, 6, :].rearrange("p (k s) -> p k s", k=TT)).then_inc(sem["pT_ready"], 1)
                sum_halves(0, n)
                scale_tokens(0, n, zt(0)).then_inc(z_scaled[0], 1)
                split_lo(1, q2)
                dve.wait_ge(sem["o_squared"], h1)
                nc.vector.tensor_scalar(var[:, 2:4], ss[:, 2:4], 1.0 / P, SUBLN_EPS, ALU.mult, ALU.add).then_inc(sem["o_var"], 1)
                split_lo(2, q2)
                dve.wait_ge(sem["oT_hi"], h1)
                nc.vector.scalar_tensor_tensor(oT[:, 1, bass.ds(h, 1), :], ps[:, 6:7, 0:S], gain[:, 0:1],
                                               oT[:, 0, bass.ds(h, 1), :].bitcast(F32), ALU.mult, ALU.subtract).then_inc(sem["oT_lo"], 1)
                sum_halves(1, n)
                scale_tokens(1, n, zt(1)).then_inc(z_scaled[1], 1)

            for i, c in enumerate((slice(0, PC // 2), slice(PC // 2, PC))):
                dve.wait_ge(sem["yp_hi"], i + 1)
                nc.vector.tensor_tensor(yp[:, 1, c, :], pooled[:, c, :], yp[:, 0, c, :].bitcast(F32), ALU.subtract).then_inc(sem["yp_lo"], 1)
            dve.wait_ge(sem["gate_ready"], 16)
            def branch_quad(q, before_last=None):
                q1, q2 = value(dve, q + 1), value(dve, q + 2)
                n, m = value(dve, q - 1), value(dve, q - Q_BRANCH + 1)
                m1 = value(dve, q - Q_BRANCH + 2)
                a1 = [value(dve, (q - Q_BRANCH) * 2 + (1 + s)) for s in range(2)]

                def gate(g, count, tile, done):
                    dve.wait_ge(bank_free[g], count)
                    nc.vector.scalar_tensor_tensor(zt(g % 2), gates[:, bass.ds(tile, 2), :], 1.0, zt(g % 2),
                                                   ALU.add, ALU.mult).then_inc(sem[f"gated{g % 2}"], 1)
                    dve.wait_ge(sem[f"gated{g % 2}"], done)

                for s in range(2):
                    split_lo(3 if s == 0 else 1, q1 if s == 0 else q2)
                    tile = value(dve, (q - Q_BRANCH) * 4 + 2 * s)
                    tile2 = value(dve, (q - Q_BRANCH) * 4 + (2 * s + KC))
                    sum_halves(2 * s, n if s == 0 else m)
                    gate(2 * s, n if s == 0 else m1, tile, a1[s])
                    split_lo(2 * s, q2)
                    if s and before_last:
                        before_last()
                    sum_halves(2 * s + 1, n if s == 0 else m)
                    gate(2 * s + 1, n if s == 0 else m1, tile2, a1[s])
                    nc.vector.tensor_tensor(merged[:, bass.ds(tile, 2), :], zt(0), zt(1), ALU.add).then_inc(sem["merged_ready"], 1)
                    dve.wait_ge(sem["merged_ready"], a1[s])

            def chunk_lo(slot, src, scale):
                return nc.vector.scalar_tensor_tensor(chunk[:, slot:slot + 1, 1, :], src, scale, chunk[:, slot:slot + 1, 0, :].bitcast(F32),
                                                      ALU.mult, ALU.subtract)

            def first_chunks(src, scale, done):
                for slot in range(3):
                    dve.wait_ge(sem["first_hi"], done + slot + 1)
                    chunk_lo(slot, src[:, slot:slot + 1, :], scale).then_inc(sem["first_lo"], 1)

            def row_phase(src, scale, first, last):
                with dve.Fori(first, last - 1) as q:
                    q1, q2 = dve.snap(q + 1), dve.snap(q + 2)
                    k = [dve.snap((q - first) * SLOTS + 3 + s) for s in range(SLOTS)]
                    for i, slot in enumerate((3, 0, 1, 2)):
                        dve.wait_ge(w_hi_ready[slot], q1 if slot == 3 else q2)
                        chunk_lo(slot, src[:, bass.ds(k[i], 1), :], scale)
                        split_lo(slot, q1 if slot == 3 else q2)
                dve.wait_ge(w_hi_ready[3], last)
                chunk_lo(3, src[:, SLOTS * (last - first) - 1:SLOTS * (last - first), :], scale)
                split_lo(3, last)

            with dve.Fori(Q_BRANCH, Q_OUT - 1) as q:
                branch_quad(q)
            branch_quad(Q_OUT - 1, before_last=lambda: first_chunks(merged, 0.5, 0))
            row_phase(merged, 0.5, Q_OUT, Q_UP)

            def row_variance(u, col, name):
                dve.wait_ge(sem[f"{name}_squared"], 4 * u + 4)
                at = ysum[:, (col // 12) * 2 + u:(col // 12) * 2 + u + 1]
                nc.vector.tensor_reduce(at, ss[:, col + 4 * u:col + 4 * u + 4], AX.X, ALU.add).then_inc(sem[f"{name}_summed"], 1)
                dve.wait_ge(sem[f"{name}_summed"], u + 1)
                r = 4 + (col // 12) * 2 + u
                nc.vector.tensor_scalar(var[:, r:r + 1], at, 1.0 / D, EPS, ALU.mult, ALU.add).then_inc(sem[f"{name}_var"], 1)
                dve.wait_ge(sem[f"{name}_rstd"], u + 1)
                return rstd[:, r:r + 1]

            def scale_y(u, b, factor, name):
                nc.vector.scalar_tensor_tensor(ybuf[:, u, WB * b:WB * (b + 1)], ps[:, 4 * u + b, :], factor,
                                               grow[:, WB * b:WB * (b + 1)], ALU.mult, ALU.mult).then_inc(sem[f"{name}_scaled"], 1)

            def add_x(u, b, name, count, done):
                dve.wait_ge(sem[f"{name}_scaled"], count)
                nc.vector.tensor_tensor(xrow[:, u, WB * b:WB * (b + 1)], ybuf[:, u, WB * b:WB * (b + 1)],
                                        xrow[:, u, WB * b:WB * (b + 1)], ALU.add).then_inc(sem[done], 1)

            def x1T_lo(u, b):
                dve.wait_ge(sem["x1T_hi"], 4 * u + b + 1)
                nc.vector.tensor_tensor(xT[:, 1, 4 * b:4 * b + 4, u * P:(u + 1) * P], ps[:, 4 * u + b, :].rearrange("p (k s) -> p k s", k=4),
                                        xT[:, 0, 4 * b:4 * b + 4, u * P:(u + 1) * P].bitcast(F32), ALU.subtract).then_inc(sem["x1T_lo"], 1)

            dve.wait_ge(sem["xrow_loaded"], 16)
            dve.wait_ge(sem["grow_loaded"], 16)
            factor = row_variance(0, 4, "y")
            for b in range(4):
                scale_y(0, b, factor, "y")
                if b < 2:
                    add_x(0, b, "y", b + 1, "x1_ready")
            split_lo(0, Q_UP + 1)
            split_lo(1, Q_UP + 1)
            x1T_lo(0, 0)
            factor = row_variance(1, 4, "y")
            scale_y(1, 0, factor, "y")
            add_x(1, 0, "y", 5, "x1_ready")
            dve.wait_ge(sem["x1_ready"], 3)
            dve.wait_ge(sem["g2row_loaded"], 16)
            nc.vector.tensor_tensor(ybuf[:, 1, 0:WB], xrow[:, 1, 0:WB], g2row[:, 0:WB], ALU.mult).then_inc(sem["x1g_first"], 1)
            scale_y(1, 1, factor, "y")
            add_x(1, 1, "y", 6, "x1_ready")
            for b in range(1, 4):
                x1T_lo(0, b)
                x1T_lo(1, b - 1)
                if b < 3:
                    scale_y(1, b + 1, factor, "y")
                    add_x(1, b + 1, "y", 6 + b, "x1_ready")
            x1T_lo(1, 3)
            split_lo(2, Q_UP + 1)
            variance("x1_squared", TT, 0, 2, D, EPS, "x1_var")
            dve.wait_ge(sem["x1_rstd"], 1)
            for u in range(TT):
                ins = nc.vector.tensor_scalar(diag[:, u * P:(u + 1) * P], ident, rstd[:, u:u + 1], None, ALU.mult)
            ins.then_inc(sem["diag_ready"], 1)

            def up_quad(q, is_first=False, before_last=None):
                q1, q2, n, i1 = value(dve, q + 1), value(dve, q + 2), value(dve, q - 5), value(dve, q - Q_UP + 1)
                taps_done = [value(dve, (q - Q_UP) * 4 + (GATED0 + k)) for k in (1, 3, 4)]

                def conv(g):
                    dve.wait_ge(sem[f"tap{g}"], i1)
                    done = sem[f"gated{g}"]
                    for j in range(2):
                        ft = value(dve, (q - Q_UP) * 2 + (FC * g + j))
                        nc.vector.scalar_tensor_tensor(tmp[g][:, j, :], z[g][:, j, 0:S], column("w0", ft), tmp[g][:, j, :],
                                                       ALU.mult, ALU.add).then_inc(done, 1)
                        dve.wait_ge(done, taps_done[j])
                        nc.vector.scalar_tensor_tensor(tmp[g][:, j, :], z[g][:, j, 2:S + 2], column("w2", ft), tmp[g][:, j, :],
                                                       ALU.mult, ALU.add).then_inc(done, 1)

                split_lo(3, q1)
                split_lo(0, q2)
                sum_halves(0, n)
                if is_first:
                    dve.wait_ge(sem["R_ready"], 2)
                scale_tokens(0, n, zt(0)).then_inc(z_scaled[0], 1)
                split_lo(1, q2)
                conv(0)
                split_lo(2, q2)
                if before_last:
                    before_last()
                sum_halves(1, n)
                scale_tokens(1, n, zt(1)).then_inc(z_scaled[1], 1)
                conv(1)
                dve.wait_ge(sem["gated1"], taps_done[2])
                dve.wait_ge(sem["gelu_ready"], i1)
                tile = value(dve, (q - Q_UP) * 2)
                nc.vector.tensor_tensor(hidden[:, bass.ds(tile, 2), :], G[:, :, :], tmp[1][:, :, :], ALU.mult).then_inc(sem["act_ready"], 1)

            up_quad(Q_UP, is_first=True)
            with dve.Fori(Q_UP + 1, Q_DOWN - 1) as q:
                up_quad(q)
            up_quad(Q_DOWN - 1, before_last=lambda: first_chunks(hidden, 1.0, 3))
            dve.wait_ge(sem["act_ready"], Q_DOWN - Q_UP)
            row_phase(hidden, 1.0, Q_DOWN, Q_END)
            dve.wait_ge(sem["grow2_loaded"], 16)
            for u in range(TT):
                factor = row_variance(u, 12, "y2")
                scale_y(u, 3, factor, "y2")
                for b in range(3):
                    scale_y(u, b, factor, "y2")
                    add_x(u, b, "y2", 4 * u + b + 2, "out_ready")

        @block.tensor
        def _(pe):
            def ready(slot, q1):
                pe.wait_ge(w_hi_ready[slot], q1)
                pe.wait_ge(w_lo_ready[slot], q1)

            def column_piece(slot, q1, g, moving, c0, last, first=True, half=None, chunk_wait=None):
                if half != 0:
                    ready(slot, q1)
                for k in range(GK) if half is None else range(4 * half, 4 * half + 4):
                    c = c0 + k
                    if chunk_wait:
                        chunk_wait(c)
                    for j in range(2):
                        col = slice(k * S + j * P, k * S + (j + 1) * P)
                        nc.tensor.matmul(ps[:, 2 * g + j, :].rearrange("p (a s) -> p a s", a=2), w_hi[slot][:, col], moving[:, :, c, :],
                                         start=(k == 0 and first), stop=False, skip_group_check=True)
                        ins = nc.tensor.matmul(ps[:, 2 * g + j, 0:S], w_lo[slot][:, col], moving[:, 0, c, :],
                                               start=False, stop=(k == GK - 1 and last), skip_group_check=True)
                if half != 0:
                    ins.then_inc(w_used[slot], 1)

            def token_piece(slot, u, moving_of, stationary_of, bank_of, groups, first, last, before=None):
                for w, hl in ((w_hi, 0), (w_lo, 0), (w_hi, 1)):
                    for g in range(groups):
                        if before and w is w_hi and hl == 0:
                            before(g)
                        ins = nc.tensor.matmul(ps[:, bank_of(g), :], stationary_of(hl), moving_of(w, g),
                                               start=(first and w is w_hi and hl == 0), stop=(last and hl == 1),
                                               skip_group_check=True)
                return ins

            def turn_x(i):
                pe.wait_ge(sem[f"x_loaded{i}"], 16)
                if i == 3:
                    pe.wait_ge(sem["xT_lo"], 4)
                for k in range(4):
                    for u in range(TT):
                        ins = nc.tensor.transpose(ps[:, turn_bank(4 * i + k), (k % 2) * S + u * P:(k % 2) * S + (u + 1) * P],
                                                  xs[:, u, (4 * i + k) * P:(4 * i + k + 1) * P], ident)
                ins.then_inc(sem["xT_turned"], 1)

            def spread_R():
                nc.tensor.matmul(ps[:, 7, 0:S], ones[:, :], diag, start=True, stop=True).then_inc(sem["R_summed"], 1)

            pe.wait_ge(sem["const_loaded"], 16)
            for i in range(4):
                turn_x(i)
            pe.wait_ge(sem["first_w_lo"], 1)
            column_piece(0, 1, 0, xT, 0, False, half=0)
            pe.wait_ge(sem["xT_lo"], 8)
            column_piece(0, 1, 0, xT, 0, False, half=1)
            pe.wait_ge(sem["xT_lo"], KC)
            column_piece(1, 1, 0, xT, GK, True, first=False)
            column_piece(2, 1, 1, xT, 0, False)
            pe.wait_ge(sem["diag_ready"], 1)
            spread_R()
            column_piece(3, 1, 1, xT, GK, True, first=False)
            with pe.Fori(1, Q_V) as q:
                q1 = pe.snap(q + 1)
                for g in range(2):
                    pe.wait_ge(bank_free[g], q)
                    column_piece(2 * g, q1, g, xT, 0, False)
                    column_piece(2 * g + 1, q1, g, xT, GK, True, first=False)

            for q in range(Q_V, Q_GATE):
                pe.wait_ge(bank_free[q - Q_V], Q_V)
                for slot in range(SLOTS):
                    if q == Q_GATE - 1 and slot == 2:
                        pe.wait_ge(sem["poolw_loaded"], 16)
                        for grp in range(4):
                            pe.wait_ge(sem["mixed_ready"], grp + 1)
                            for j in range(2):
                                for k in range(2):
                                    ins = nc.tensor.matmul(ps[:, 4 + grp, j * S:(j + 1) * S], pw[:, grp, k, j * P:(j + 1) * P],
                                                           mixed[:, 2 * grp + k, :], start=(k == 0), stop=(k == 1), skip_group_check=True)
                            ins.then_inc(sem["pooled"], 1)
                    ready(slot, q + 1)
                    for k in range(4):
                        c = 4 * slot + k
                        for u in range(TT):
                            ins = token_piece(slot, u, lambda w, g: w[slot][:, WB * k:WB * (k + 1)],
                                              lambda hl: xT[:, hl, c, u * P:(u + 1) * P],
                                              lambda g: 2 * (q - Q_V) + u, 1, c == 0, c == KC - 1)
                    ins.then_inc(w_used[slot], 1)

            pe.wait_ge(bank_free[2], 1)
            pe.wait_ge(bank_free[3], 1)
            with pe.Fori(Q_GATE, Q_BRANCH) as q:
                q1, nf, h1 = pe.snap(q + 1), pe.snap(q - 2), pe.snap(q - Q_GATE + 1)
                hu2 = pe.snap((q - Q_GATE) * 2 + 2)
                pe.wait_ge(sem["head_qk"], h1)
                for c in range(2):
                    rows = slice(c * HD, (c + 1) * HD)
                    for u in range(TT):
                        ins = nc.tensor.matmul(ps[:, 4 + c, u * S:(u + 1) * S], qk_head[rows, 0, u * P:(u + 1) * P],
                                               qk_head[rows, 1, :], start=True, stop=True, skip_group_check=True)
                ins.then_inc(sem["scores_done"], 1)
                pe.wait_ge(sem["v_ready"], 2)
                pe.wait_ge(bank_free[0], nf)
                column_piece(0, q1, 0, xT, 0, False)
                column_piece(1, q1, 0, xT, GK, True, first=False)
                pe.wait_ge(sem["probs_ready"], hu2)
                for u in range(TT):
                    for k in range(TT):
                        ins = nc.tensor.transpose(ps[:, 6, k * S + u * P:k * S + (u + 1) * P], probs[:, u, k * P:(k + 1) * P], ident)
                ins.then_inc(sem["pT_turned"], 1)
                pe.wait_ge(sem["v_ready"], 4)
                pe.wait_ge(bank_free[1], nf)
                column_piece(2, q1, 1, xT, 0, False)
                pe.wait_ge(sem["pT_ready"], h1)
                pe.wait_ge(sem["head_v"], h1)
                for u in range(TT):
                    for k in range(TT):
                        ins = nc.tensor.matmul(ps[:, 7, u * P:(u + 1) * P], pT[:, k, u * P:(u + 1) * P], v_head[:, k, :],
                                               start=(k == 0), stop=(k == TT - 1), skip_group_check=True)
                ins.then_inc(sem["o_done"], 1)
                column_piece(3, q1, 1, xT, GK, True, first=False)
                pe.wait_ge(sem["o_scaled"], h1)
                for u in range(TT):
                    ins = nc.tensor.transpose(ps[:, 6, u * P:(u + 1) * P], o[:, u, :], ident)
                ins.then_inc(sem["oT_turned"], 1)

            def head_ready(c):
                if c in (0, HEADS - 1):
                    pe.wait_ge(sem["oT_lo"], HEADS - (c == 0))

            def pooled_ready(c):
                if c in (0, PC // 2):
                    pe.wait_ge(sem["yp_lo"], 1 + c // (PC // 2))

            with pe.Fori(Q_BRANCH, Q_OUT) as q:
                q1, nf, mf = pe.snap(q + 1), pe.snap(q - 2), pe.snap(q - Q_BRANCH + 1)
                for g in range(4):
                    pe.wait_ge(bank_free[g], nf if g < 2 else mf)
                    column_piece(g, q1, g, yp if g % 2 else oT, 0, True, chunk_wait=pooled_ready if g % 2 else head_ready)

            def row_piece(slot, u, first, last, before=None):
                return token_piece(slot, u, lambda w, g: w[slot][:, WB * g:WB * (g + 1)],
                                   lambda hl: chunk[:, slot, hl, u * P:(u + 1) * P],
                                   lambda g: 4 * u + g, 4, first, last, before)

            def row_phase(first, last, done, order, bank_wait, first_chunks, between=None):
                def quad(q1, is_first):
                    for slot in range(SLOTS):
                        ready(slot, q1)
                        if is_first and slot < 3:
                            pe.wait_ge(sem["first_lo"], first_chunks + slot + 1)
                        for u in order:
                            ins = row_piece(slot, u, is_first and slot == 0, False,
                                            before=(lambda g: bank_wait(u, g)) if is_first and slot == 0 else None)
                        ins.then_inc(w_used[slot], 1)

                quad(first + 1, True)
                with pe.Fori(first + 1, last - 1) as q:
                    quad(pe.snap(q + 1), False)
                for u in range(TT):
                    for slot in range(SLOTS):
                        if u == 0:
                            ready(slot, last)
                        if between and u == 1 and slot == 3:
                            between()
                        if slot < 3:
                            ins = row_piece(slot, u, False, False)
                            if u == 1:
                                ins.then_inc(w_used[slot], 1)
                        else:
                            for g in range(4):
                                for w, hl in ((w_hi, 0), (w_lo, 0), (w_hi, 1)):
                                    ins = nc.tensor.matmul(ps[:, 4 * u + g, :], chunk[:, slot, hl, u * P:(u + 1) * P],
                                                           w[slot][:, WB * g:WB * (g + 1)], start=False, stop=(hl == 1),
                                                           skip_group_check=True)
                                if u == 1 and g == 3:
                                    ins.then_inc(w_used[slot], 1)
                                else:
                                    ins.then_inc(done, 1)

            def turn_x1(u, b):
                if (u, b) == (1, 0):
                    pe.wait_ge(sem["x1g_first"], 1)
                else:
                    pe.wait_ge(sem[f"x1g_ready{u}"], b + 1 - u)
                for k in range(4):
                    c = 4 * b + k
                    ins = nc.tensor.transpose(ps[:, 4 * u + b, k * P:(k + 1) * P], ybuf[:, u, c * P:(c + 1) * P], ident)
                ins.then_inc(sem["x1_turned"], 1)

            def after_branches(u, g):
                if g % 2 == 0:
                    grp = 2 * u + g // 2
                    pe.wait_ge(bank_free[grp], 18 if grp < 2 else 5)

            row_phase(Q_OUT, Q_UP, sem["y_done"], (0, 1), after_branches, 0,
                      between=lambda: [turn_x1(0, b) for b in range(2)])
            for b in range(2, 4):
                turn_x1(0, b)

            def turned(c):
                b, first = divmod(c, 4)
                if first == 0:
                    if b < 3:
                        turn_x1(1, b + 1)
                    pe.wait_ge(sem["x1T_lo"], (3, 5, 7, 8)[b])

            turn_x1(1, 0)

            column_piece(0, Q_UP + 1, 0, xT, 0, False, chunk_wait=turned)
            column_piece(1, Q_UP + 1, 0, xT, GK, True, first=False, chunk_wait=turned)
            pe.wait_ge(sem["diag_ready"], 2)
            spread_R()
            column_piece(2, Q_UP + 1, 1, xT, 0, False)
            column_piece(3, Q_UP + 1, 1, xT, GK, True, first=False)
            with pe.Fori(Q_UP + 1, Q_DOWN) as q:
                q1, nf = pe.snap(q + 1), pe.snap(q - 6)
                for g in range(2):
                    pe.wait_ge(bank_free[g], nf)
                    column_piece(2 * g, q1, g, xT, 0, False)
                    column_piece(2 * g + 1, q1, g, xT, GK, True, first=False)

            def after_up(u, g):
                if u == 0 and g % 2 == 0:
                    pe.wait_ge(bank_free[g // 2], Q_DOWN - 6)

            row_phase(Q_DOWN, Q_END, sem["y2_done"], (1, 0), after_up, 3)


GATED0 = 8


def kernel(**inputs):
    import numpy as np
    import concourse.bacc as bacc
    from concourse.bass_utils import run_bass_kernel_spmd

    def feature_columns(a):
        return np.ascontiguousarray(a.reshape(-1, P).T)

    g = {k: np.asarray(a) for k, a in inputs.items()}
    conv = g["conv_w"][0]
    params = np.concatenate([feature_columns(a) for a in (
        g["g_pre_mix"][0], g["b_gate"][0], g["pool_scale"][0], g["subln_gain"][0],
        conv[0], conv[1], conv[2], g["conv_b"][0])], axis=1)
    lambdas = np.concatenate([g["lambda_q1"], g["lambda_k1"], g["lambda_q2"], g["lambda_k2"]], axis=1)

    keys = np.arange(S)
    dist = np.abs(np.arange(P)[:, None, None] + P * np.arange(TT)[None, :, None] - keys[None, None, :])
    slopes = np.array([-(2.0 ** (-8.0 * (h + 1) / HEADS)) / SCALE for h in range(HEADS)])
    consts = np.concatenate([np.eye(P), dist.reshape(P, TT * S), np.tile(slopes, (P, 1))], axis=1).astype(np.float32)
    counts = np.stack([np.minimum(keys + w // 2, S) - np.maximum(keys - w // 2, 0) for w in WINDOWS])
    invcnt = np.ascontiguousarray(np.broadcast_to((1.0 / counts).reshape(1, -1), (P, 4 * S)).astype(np.float32))

    arrays = {"x": g["x"][0], "w_in": g["w_in"][0], "w_attn_branch": g["w_attn_branch"][0], "pool_w": g["pool_w"][0],
              "w_pool_branch": g["w_pool_branch"][0], "w_out": g["w_out"][0], "w_up": g["w_up"][0], "w_down": g["w_down"][0],
              "g_post_mix": g["g_post_mix"], "g_pre_ffn": g["g_pre_ffn"], "g_post_ffn": g["g_post_ffn"], "lambdas": lambdas, "params": params,
              "consts": consts, "invcnt": invcnt}
    arrays = {k: np.ascontiguousarray(a) for k, a in arrays.items()}
    nc = bacc.Bacc("TRN2", target_bir_lowering=False, num_devices=1, dynamic_dma_scratch_size=1024)
    args = [nc.dram_tensor(f"in_{k}", a.shape, F32, kind="ExternalInput").ap() for k, a in arrays.items()]
    out = nc.dram_tensor("out", (S, D), F32, kind="ExternalOutput").ap()
    build(nc, *args, out)
    r = run_bass_kernel_spmd(nc, [{f"in_{k}": a for k, a in arrays.items()}], core_ids=[0])
    return r.results[0]["out"].reshape(1, S, D)
```

```python
from contextlib import ExitStack
import math

import numpy as np

import concourse.bass as bass
from concourse import mybir

F32 = mybir.dt.float32
F32R = mybir.dt.float32r
ACT = mybir.ActivationFunctionType
ALU = mybir.AluOpType
AX = mybir.AxisListType

P = 128
D = 2048
S = 256
TT = S // P
KC = D // P
HEADS = 8
HD = 64
AW = HEADS * 2 * HD
PW = D // 2
PC = PW // P
WINDOWS = (2, 4, 8, 16)
PAD = max(WINDOWS) // 2
PROW = S + 2 * PAD
DFF = (11 * D // 4) // P * P
FC = DFF // P
EPS = 1e-6
SUBLN_EPS = 1e-5
SCALE = HD ** -0.5
LAMBDA_INIT = 0.8 - 0.6 * math.exp(0.0)
PIECE = 2048
SLOTS = 4
GK = PIECE // S
WB = 512

Q_P = 4
Q_V = Q_P + 2
Q_GATE = Q_V + 2
Q_BRANCH = Q_GATE + 8
Q_OUT = Q_BRANCH + 4
Q_UP = Q_OUT + KC // SLOTS
Q_DOWN = Q_UP + FC // 2
Q_END = Q_DOWN + FC // SLOTS

COL = {}
_at = 0
for _name, _n in (("g_pre_mix", KC), ("b_gate", 2 * KC), ("pool_scale", PC),
                  ("subln_gain", 1), ("w0", 2 * FC), ("w1", 2 * FC), ("w2", 2 * FC), ("conv_b", 2 * FC)):
    COL[_name] = (_at, _n)
    _at += _n
NPAR = _at
YP_PARTS = [slice(c, c + 2) for c in range(0, PC, 2)]
C_ID, C_DIST, C_SLOPE = 0, P, P + TT * S
NCONST = C_SLOPE + HEADS

SEMAPHORES = (
    [f"{n}{s}" for n in ("w_loaded", "w_hi_ready", "w_lo_ready", "w_used") for s in range(SLOTS)]
    + [f"{n}{g}" for n in ("half_copied", "bank_free") for g in range(4)]
    + [f"x_loaded{i}" for i in range(4)] + [f"z_scaled{g}" for g in range(2)]
    + ["ident_loaded", "dist_loaded", "conv_loaded", "par_loaded", "lam_loaded", "invcnt_loaded", "poolw_loaded", "xrow_loaded",
       "grow_loaded", "g2row_loaded", "grow2_loaded", "first_loaded", "first_w_hi", "first_w_lo", "out_stored",
       "ones_set", "pads_set", "half_set",
       "xT_turned", "xT_hi", "xT_lo", "x_squared", "x_var", "x_rstd", "diag_ready", "R_summed", "R_ready",
       "lam_prod", "lam_sum", "lam_exp", "lam_ready", "gain_scaled", "bias_halved",
       "p_ready", "window_step", "mixed_ready", "pooled", "v_ready",
       "head_copied", "head_qk", "head_v", "scores_done", "t_biased", "t_max", "exp_done", "sum_inv", "lam_inv",
       "p1_scaled", "probs_ready", "pT_turned", "pT_ready", "o_done", "o_squared", "o_var", "o_rstd",
       "o_scaled", "oT_turned", "oT_hi", "oT_lo", "neg_max", "gate_ready", "yp_hi", "yp_lo",
       "gated0", "gated1", "merged_ready", "first_hi", "first_lo", "y_done", "y_squared", "y_var",
       "y_rstd", "y_gained", "x1_ready", "x1_turned", "x1T_hi", "x1T_lo", "x1g_ready0", "x1g_ready1", "x1g_first", "y_summed", "x1_squared", "x1_var",
       "x1_rstd", "tap0", "tap1", "gelu_ready", "out_pool", "act_ready", "y2_done", "y2_squared",
       "y2_summed", "y2_var", "y2_rstd", "y2_gained", "y2_scaled", "out_ready"])


def build(nc, x, w_in, w_attn_branch, pool_w, w_pool_branch, w_out, w_up, w_down,
          g_post_mix, g_pre_ffn, g_post_ffn, lambdas, params, consts, invcnt, out):
    with ExitStack() as ctx:
        place = [(nc.sbuf_base + 31) // 32 * 32]
        spans = {}

        def sb(name, shape, dt=F32, at=None):
            size = int(np.prod(shape[1:])) * 4
            if at is None:
                at = place[0]
                place[0] += (size + 31) // 32 * 32
            assert at + size <= 229344, (name, at + size)
            spans[name] = at
            return nc.alloc_sbuf_tensor_at(name, shape, dt, offset=at)

        w_raw = [sb(f"w_raw{s}", [P, PIECE]) for s in range(SLOTS)]
        w_hi = [sb(f"w_hi{s}", [P, PIECE], F32R) for s in range(SLOTS)]
        w_lo = [sb(f"w_lo{s}", [P, PIECE], F32R) for s in range(SLOTS)]
        xT = sb("xT", [P, 2, KC, S], F32R)
        tmp = [sb(f"tmp{g}", [P, 2, S]) for g in range(2)]
        z = [sb(f"z{g}", [P, 2, S + 2]) for g in range(2)]
        cst = sb("cst", [P, NCONST])
        par = sb("par", [P, NPAR])
        ones = sb("ones", [P, P])
        R = sb("R", [P, 1, S])
        ss = sb("ss", [P, 20])
        ysum = sb("ysum", [P, 4])
        var = sb("var", [P, 8])
        rstd = sb("rstd", [P, 8])
        half = sb("half", [P, 2])
        hbias = sb("hbias", [P, 2 * KC])
        gain = sb("gain", [P, 1])
        small = sb("small", [P, 32])
        U = place[0]
        qk = sb("qk", [P, 2, HEADS, S])
        v = sb("v", [P, TT, AW])
        ppad = sb("ppad", [P, PC, PROW])
        gates = sb("gates", [P, 2 * KC, S])
        t = [sb(f"t{u}", [P, 2, S]) for u in range(TT)]
        probs = sb("probs", [P, TT, S])
        pT = sb("pT", [P, TT, S])
        qk_now = sb("qk_now", [P, 2, S])
        qk_head = sb("qk_head", [P, 2, 2, S], F32R)
        v_head = sb("v_head", [P, TT, P])
        o = sb("o", [P, TT, P])
        oT = sb("oT", [P, 2, HEADS, S], F32R, at=spans["qk"])
        pooled = sb("pooled", [P, PC, S], at=spans["ppad"])
        xs = sb("xs", [P, TT, D], at=spans["gates"])
        junk = sb("junk", [P, D], at=spans["gates"] + 16384)
        mixed = sb("mixed", [P, PC, S], at=spans["gates"])
        win = [sb(f"win{i}", [P, 2, PROW], at=spans["gates"] + 8192 + 2176 * i) for i in range(2)]
        icnt = sb("icnt", [P, 4, 1, S], at=spans["gates"] + 16384 + 2048 * 2)
        pw = sb("pw", [P, 4, 2, S], at=spans["gates"] + 24576)
        lamv = sb("lamv", [P, 2, 2, HD], at=spans["probs"])
        lamp = sb("lamp", [P, 2, HD], at=spans["probs"] + 1024)
        yp = sb("yp", [P, 2, PC, S], F32R, at=spans["xT"])
        merged = sb("merged", [P, KC, S], at=spans["xT"] + 16384)
        place[0] = U
        chunk = sb("chunk", [P, SLOTS, 2, S], F32R)
        G = sb("G", [P, 2, S])
        grow = sb("grow", [P, D])
        xrow = sb("xrow", [P, TT, D])
        hidden = sb("hidden", [P, FC, S])
        ybuf = sb("ybuf", [P, TT, D], at=spans["hidden"])
        junk2 = sb("junk2", [P, D], at=spans["hidden"] + 16384)
        g2row = sb("g2row", [P, D], at=spans["hidden"] + 24576)

        ps = ctx.enter_context(nc.psum_tensor("ps", [P, 8, WB], F32))
        sem = {n: ctx.enter_context(nc.semaphore(n)) for n in SEMAPHORES}
        w_loaded, w_hi_ready, w_lo_ready, w_used = (
            [sem[f"{n}{s}"] for s in range(SLOTS)] for n in ("w_loaded", "w_hi_ready", "w_lo_ready", "w_used"))
        half_copied, bank_free = (
            [sem[f"{n}{g}"] for g in range(4)] for n in ("half_copied", "bank_free"))
        z_scaled = [sem["z_scaled0"], sem["z_scaled1"]]

        ident = cst[:, C_ID:C_ID + P]
        dist = cst[:, C_DIST:C_DIST + TT * S].rearrange("p (u o k) -> p u o k", u=TT, o=1)
        diag = tmp[1][:, 0, :]
        rmax = small[:, 0:4].rearrange("p (u c) -> p u c", u=TT)
        nmax = small[:, 4:8].rearrange("p (u c) -> p u c", u=TT)
        esum = small[:, 8:12].rearrange("p (u c) -> p u c", u=TT)
        einv = small[:, 12:16].rearrange("p (u c) -> p u c", u=TT)
        linv = small[:, 16:18]
        lsum = small[:, 18:20]
        lexp = small[:, 20:22]
        lam = small[:, 22:23]

        def column(name, n=0):
            return par[:, bass.ds(COL[name][0] + n, 1)] if not isinstance(n, int) else \
                par[:, COL[name][0] + n:COL[name][0] + n + 1]

        def zt(g):
            return z[g][:, :, 1:S + 1]

        def turn_bank(c):
            return (4, 5, 6, 7, 2, 3, 4, 5)[c // 2]

        def pair(g, half_no):
            return ps[:, 2 * g:2 * g + 2, half_no * S:(half_no + 1) * S]

        def value(eng, n):
            return n if isinstance(n, int) else eng.snap(n)

        def quad_values(eng, q):
            return value(eng, q + 1), value(eng, q + 2), value(eng, q * 16 + 16), value(eng, q * 16 + 32)

        block = ctx.enter_context(nc.Block())

        @block.sync
        def _(sp):
            def columns(w, h, col):
                return w.rearrange("(h k p) n -> h p k n", p=P, k=GK)[h, :, :, bass.ds(col, S)]

            def load(slot, q, src, first=False):
                if not first:
                    sp.wait_ge(w_lo_ready[slot], q)
                n = src.shape[-1]
                sp.dma_start(w_raw[slot][:, :].rearrange("p (k n) -> p k n", n=n) if len(src.shape) == 3
                             else w_raw[slot][:, :], src).then_inc(w_loaded[slot], 16)

            x_v = x.rearrange("(u p) d -> p u d", p=P)

            def load_x(i):
                sp.dma_start(xs[:, :, WB * i:WB * (i + 1)], x_v[:, :, WB * i:WB * (i + 1)]).then_inc(sem[f"x_loaded{i}"], 16)

            load_x(0)
            first_half = w_raw[0][:, :].rearrange("p (a k n) -> p a k n", a=2, n=S)
            first_src = columns(w_in, 0, 0).rearrange("p (a k) n -> p a k n", a=2)
            sp.dma_start(first_half[:, 0, :, :], first_src[:, 0, :, :]).then_inc(sem["first_loaded"], 16)
            load_x(1)
            sp.dma_start(first_half[:, 1, :, :], first_src[:, 1, :, :]).then_inc(w_loaded[0], 16)
            load_x(2)
            load_x(3)
            sp.dma_start(lamv[:, :, :, :].rearrange("p a b d -> p (a b d)"), lambdas.to_broadcast([P, 4 * HD])).then_inc(sem["lam_loaded"], 16)
            load(1, 0, columns(w_in, 1, 0), first=True)
            load(2, 0, columns(w_in, 0, S), first=True)
            load(3, 0, columns(w_in, 1, S), first=True)
            sp.dma_start(cst[:, C_DIST:], consts[:, C_DIST:]).then_inc(sem["dist_loaded"], 16)
            sp.dma_start(par[:, COL["w0"][0]:], params[:, COL["w0"][0]:]).then_inc(sem["conv_loaded"], 16)

            def in_quads(first, last, col0):
                with sp.Fori(first, last) as q:
                    c0 = sp.snap((q - first) * (2 * S) + col0)
                    c1 = sp.snap((q - first) * (2 * S) + col0 + S)
                    for slot in range(SLOTS):
                        load(slot, q, columns(w_in, slot % 2, c0 if slot < 2 else c1))

            in_quads(1, Q_P, 2 * S)
            in_quads(Q_P, Q_V, 3 * AW)
            sp.wait_ge(sem["x_squared"], TT)
            sp.wait_ge(sem["xT_lo"], KC)
            sp.dma_start(icnt[:, :, :, :].rearrange("p g o s -> p (g o s)"), invcnt).then_inc(sem["invcnt_loaded"], 16)
            sp.dma_start(pw[:, :, :, :].rearrange("p g k n -> p (g k) n"),
                         pool_w.rearrange("g (k p) n -> p (g k) n", p=P)).then_inc(sem["poolw_loaded"], 16)
            for q in range(Q_V, Q_GATE):
                for slot in range(SLOTS):
                    col = 2 * AW + WB * (q - Q_V)
                    load(slot, q, w_in.rearrange("(h k p) n -> h p k n", p=P, k=4)[slot, :, :, col:col + WB])
            in_quads(Q_GATE, Q_BRANCH, 3 * AW + PW)
            with sp.Fori(Q_BRANCH, Q_OUT) as q:
                c0 = sp.snap((q - Q_BRANCH) * (2 * S))
                c1 = sp.snap((q - Q_BRANCH) * (2 * S) + S)
                for slot in range(SLOTS):
                    load(slot, q, columns(w_pool_branch if slot % 2 else w_attn_branch, 0, c0 if slot < 2 else c1))

            for q in range(Q_OUT, Q_UP):
                if q == Q_OUT + 2:
                    sp.wait_ge(sem["merged_ready"], 8)
                    sp.wait_ge(w_used[3], Q_OUT)
                    sp.dma_start(xrow[:, :, :], x_v).then_inc(sem["xrow_loaded"], 16)
                if q == Q_OUT + 3:
                    sp.dma_start(grow[:, :], g_post_mix.to_broadcast([P, D])).then_inc(sem["grow_loaded"], 16)
                    sp.dma_start(g2row[:, :], g_pre_ffn.to_broadcast([P, D])).then_inc(sem["g2row_loaded"], 16)
                for slot in range(SLOTS):
                    row = P * ((q - Q_OUT) * SLOTS + slot)
                    load(slot, q, w_out[row:row + P, :])
            with sp.Fori(Q_UP, Q_DOWN) as q:
                c0 = sp.snap((q - Q_UP) * S)
                c1 = sp.snap((q - Q_UP) * S + DFF)
                for slot in range(SLOTS):
                    load(slot, q, columns(w_up, slot % 2, c0 if slot < 2 else c1))
            sp.wait_ge(sem["y_gained"], 2 * SLOTS)
            sp.dma_start(grow[:, :], g_post_ffn.to_broadcast([P, D])).then_inc(sem["grow2_loaded"], 16)
            with sp.Fori(Q_DOWN, Q_END) as q:
                rows = [sp.snap((q - Q_DOWN) * (SLOTS * P) + P * s) for s in range(SLOTS)]
                for slot in range(SLOTS):
                    load(slot, q, w_down[bass.ds(rows[slot], P), :])
            out_v = out.rearrange("(u p) d -> u p d", p=P)
            for u in range(TT):
                for b in (1, 2, 0, 3):
                    if b:
                        sp.wait_ge(sem["out_ready"], 3 * u + b)
                    else:
                        sp.wait_ge(sem["out_pool"], u + 1)
                    sp.dma_start(out_v[u, :, WB * b:WB * (b + 1)], xrow[:, u, WB * b:WB * (b + 1)]).then_inc(sem["out_stored"], 16)
            sp.wait_ge(sem["out_stored"], 16 * 4 * TT)

        @block.gpsimd
        def _(pool):
            pool.memset(half[:, :], -0.5).then_inc(sem["half_set"], 1)
            pool.memset(ppad[:, :, 0:PAD], 0.0)
            pool.memset(ppad[:, :, PAD + S:PROW], 0.0).then_inc(sem["pads_set"], 1)

            def power(var_ready, n, col, width, done):
                pool.wait_ge(sem[var_ready], n)
                nc.gpsimd.tensor_tensor(rstd[:, col:col + width], var[:, col:col + width], half[:, 0:width],
                                        ALU.pow).then_inc(sem[done], 1)

            pool.wait_ge(sem["half_set"], 1)
            power("x_var", 1, 0, 2, "x_rstd")

            steps = 0
            pool.wait_ge(sem["pads_set"], 1)
            pool.wait_ge(sem["invcnt_loaded"], 16)
            for grp, window in enumerate(WINDOWS):
                pool.wait_ge(sem["p_ready"], grp + 1)
                if grp:
                    pool.wait_ge(sem["mixed_ready"], grp)
                src = ppad[:, 2 * grp:2 * grp + 2, :]
                length, reach, at = PROW, 1, 0
                while reach < window:
                    length -= reach
                    nc.gpsimd.tensor_tensor(win[at][:, :, 0:length], src[:, :, 0:length], src[:, :, reach:reach + length],
                                            ALU.add).then_inc(sem["window_step"], 1)
                    steps += 1
                    pool.wait_ge(sem["window_step"], steps)
                    src, at, reach = win[at], 1 - at, 2 * reach
                first = PAD - window // 2
                nc.gpsimd.tensor_tensor(win[at][:, :, 0:S], src[:, :, first:first + S],
                                        icnt[:, grp, :, :].to_broadcast([P, 2, S]), ALU.mult).then_inc(sem["window_step"], 1)
                steps += 1
                pool.wait_ge(sem["window_step"], steps)
                nc.gpsimd.tensor_tensor(mixed[:, 2 * grp:2 * grp + 2, :], win[at][:, :, 0:S],
                                        ppad[:, 2 * grp:2 * grp + 2, PAD:PAD + S], ALU.subtract).then_inc(sem["mixed_ready"], 1)

            def copy_head(src):
                nc.gpsimd.tensor_copy(qk_now[:, :, :], src).then_inc(sem["head_copied"], 1)
                nc.gpsimd.tensor_copy(qk_head[:, 0, :, :], src).then_inc(sem["head_copied"], 1)

            def head_lo(copied):
                pool.wait_ge(sem["head_copied"], copied)
                nc.gpsimd.tensor_tensor(qk_head[:, 1, :, :], qk_now[:, :, :], qk_head[:, 0, :, :].bitcast(F32),
                                        ALU.subtract).then_inc(sem["head_qk"], 1)

            copy_head(qk[:, :, 0, :])
            head_lo(2)
            pool.wait_ge(sem["v_ready"], 4)
            nc.gpsimd.tensor_copy(v_head[:, :, :], v[:, :, 0:P]).then_inc(sem["head_v"], 1)
            with pool.Fori(1, HEADS) as h:
                vcol, copied = pool.snap(h * P), pool.snap(h * 2 + 2)
                pool.wait_ge(sem["scores_done"], h)
                copy_head(qk[:, :, bass.ds(h, 1), :].rearrange("p a o s -> p a (o s)"))
                head_lo(copied)
                pool.wait_ge(sem["o_var"], h)
                nc.gpsimd.tensor_tensor(rstd[:, 2:4], var[:, 2:4], half[:, 0:2], ALU.pow).then_inc(sem["o_rstd"], 1)
                nc.gpsimd.tensor_copy(v_head[:, :, :], v[:, :, bass.ds(vcol, P)]).then_inc(sem["head_v"], 1)
            power("o_var", HEADS, 2, 2, "o_rstd")

            def gain_x1(u, b):
                pool.wait_ge(sem["x1_ready"], 4 * u + b + 1)
                cols = slice(WB * b, WB * (b + 1))
                nc.gpsimd.tensor_tensor(ybuf[:, u, cols], xrow[:, u, cols], g2row[:, cols], ALU.mult).then_inc(sem[f"x1g_ready{u}"], 1)

            power("y_var", 1, 4, 1, "y_rstd")
            pool.wait_ge(sem["g2row_loaded"], 16)
            for b in range(4):
                gain_x1(0, b)
            power("y_var", 2, 5, 1, "y_rstd")
            for b in range(1, 4):
                gain_x1(1, b)
            power("x1_var", 1, 0, 2, "x1_rstd")
            for u in range(TT):
                power("y2_var", u + 1, 6 + u, 1, "y2_rstd")
                pool.wait_ge(sem["y2_scaled"], u + 1)
                nc.gpsimd.tensor_tensor(xrow[:, u, 0:WB], ybuf[:, u, 0:WB], xrow[:, u, 0:WB], ALU.add).then_inc(sem["out_pool"], 1)

        @block.scalar
        def _(act):
            def split_hi(slot, q, q1, d1):
                act.wait_ge(w_loaded[slot], d1)
                if not (isinstance(q, int) and q == 0):
                    act.wait_ge(w_used[slot], q)
                nc.scalar.activation(w_hi[slot][:, :], w_raw[slot][:, :], ACT.Copy).then_inc(w_hi_ready[slot], 1)

            def copy_half(g, slot, q1):
                act.wait_ge(w_used[slot], q1)
                nc.scalar.activation(tmp[g % 2][:, :, :], pair(g, 1), ACT.Copy).then_inc(half_copied[g], 1)

            early = COL["w0"][0]
            act.dma_start(cst[:, C_ID:C_ID + P], consts[:, C_ID:C_ID + P]).then_inc(sem["ident_loaded"], 16)
            act.dma_start(par[:, 0:early], params[:, 0:early]).then_inc(sem["par_loaded"], 16)

            def turn_hi(c):
                act.wait_ge(sem["xT_turned"], c // 4 + 1)
                src = ps[:, turn_bank(c), (c % 2) * S:(c % 2 + 1) * S]
                nc.scalar.activation(xT[:, 0, c, :], src, ACT.Copy, scale=column("g_pre_mix", c)).then_inc(sem["xT_hi"], 1)

            act.wait_ge(sem["par_loaded"], 16)
            nc.scalar.mul(hbias[:, :], par[:, COL["b_gate"][0]:COL["b_gate"][0] + 2 * KC], 0.5).then_inc(sem["bias_halved"], 1)
            nc.scalar.mul(gain[:, :], column("subln_gain"), 1.0 - LAMBDA_INIT).then_inc(sem["gain_scaled"], 1)
            H = PIECE // 2
            for c in range(4):
                turn_hi(c)
            act.wait_ge(sem["first_loaded"], 16)
            nc.scalar.activation(w_hi[0][:, 0:H], w_raw[0][:, 0:H], ACT.Copy).then_inc(sem["first_w_hi"], 1)
            for c in range(4, 8):
                turn_hi(c)
            act.wait_ge(w_loaded[0], 16)
            nc.scalar.activation(w_hi[0][:, H:], w_raw[0][:, H:], ACT.Copy).then_inc(w_hi_ready[0], 1)
            for c in range(8, KC):
                turn_hi(c)

            def square_x(u):
                if u:
                    act.wait_ge(sem["x_squared"], u)
                nc.scalar.activation(junk[:, :], xs[:, u, :], ACT.Square, accum_out=ss[:, u:u + 1]).then_inc(sem["x_squared"], 1)

            act.wait_ge(w_loaded[1], 16)
            nc.scalar.activation(w_hi[1][:, 0:H], w_raw[1][:, 0:H], ACT.Copy).then_inc(sem["first_w_hi"], 1)
            nc.scalar.activation(w_hi[1][:, H:], w_raw[1][:, H:], ACT.Copy).then_inc(w_hi_ready[1], 1)
            square_x(0)
            split_hi(2, 0, 1, 16)
            square_x(1)
            act.wait_ge(sem["lam_sum"], 1)
            nc.scalar.activation(lexp, lsum, ACT.Exp).then_inc(sem["lam_exp"], 1)

            def copy_R(n):
                act.wait_ge(sem["R_summed"], n)
                nc.scalar.copy(R[:, 0, :], ps[:, 7, 0:S]).then_inc(sem["R_ready"], 1)

            def splits(q, slots):
                for slot in slots:
                    split_hi(slot, q, q + 1, 16 * (q + 1))

            for q in range(Q_V):
                splits(q, [3])
                splits(q + 1, [0])
                if q == 0:
                    copy_R(1)
                copy_half(0, 1, q + 1)
                splits(q + 1, [1, 2])
                copy_half(1, 3, q + 1)
            for q in range(Q_V, Q_GATE):
                splits(q, [3])
                splits(q + 1, [0, 1])
                if q == Q_GATE - 1:
                    for n in range(PC):
                        act.wait_ge(sem["pooled"], n // 2 + 1)
                        ins = nc.scalar.activation(pooled[:, n, :], ps[:, 4 + n // 2, (n % 2) * S:(n % 2 + 1) * S],
                                                   ACT.Copy, scale=column("pool_scale", n))
                        if n % 4 == 3:
                            ins.then_inc(bank_free[2 + n // 4], 1)
                splits(q + 1, [2])
                act.wait_ge(w_used[3], q + 1)
                for u in range(TT):
                    nc.scalar.activation(v[:, u, WB * (q - Q_V):WB * (q - Q_V + 1)], ps[:, 2 * (q - Q_V) + u, :],
                                         ACT.Copy, scale=rstd[:, u:u + 1]).then_inc(sem["v_ready"], 1)

            act.wait_ge(sem["bias_halved"], 1)
            act.wait_ge(sem["gain_scaled"], 1)
            with act.Fori(Q_GATE, Q_BRANCH) as q:
                q1, q2, d1, d2 = act.snap(q + 1), act.snap(q + 2), act.snap(q * 16 + 16), act.snap(q * 16 + 32)
                n, h, h1, hu = act.snap(q - 3), act.snap(q - Q_GATE), act.snap(q - Q_GATE + 1), act.snap((q - Q_GATE) * 2 + 1)
                hu2 = act.snap((q - Q_GATE) * 2 + 2)
                tile = act.snap((q - Q_GATE) * 4)
                for u in range(TT):
                    act.wait_ge(sem["neg_max"], hu if u == 0 else hu2)
                    for c in range(2):
                        ins = nc.scalar.activation(t[u][:, c, :], t[u][:, c, :], ACT.Exp, bias=nmax[:, u, c:c + 1],
                                                   scale=SCALE, accum_out=esum[:, u, c:c + 1])
                    ins.then_inc(sem["exp_done"], 1)
                split_hi(3, q, q1, d1)
                split_hi(0, q1, q2, d2)

                def tanh(g):
                    act.wait_ge(z_scaled[g], n)
                    for j in range(2):
                        at = act.snap(tile + (2 * g + j))
                        ins = nc.scalar.activation(gates[:, bass.ds(at, 1), :], z[g][:, j:j + 1, 1:S + 1], ACT.Tanh,
                                                   bias=hbias[:, bass.ds(at, 1)], scale=0.5)
                    ins.then_inc(sem["gate_ready"], 1)

                copy_half(0, 1, q1)
                split_hi(1, q1, q2, d2)
                tanh(0)
                act.wait_ge(sem["o_done"], h1)
                for u in range(TT):
                    ins = nc.scalar.activation(o[:, u, :], ps[:, 7, u * P:(u + 1) * P], ACT.Square, accum_out=ss[:, 2 + u:3 + u])
                ins.then_inc(sem["o_squared"], 1)
                act.wait_ge(sem["o_rstd"], h1)
                for u in range(TT):
                    ins = nc.scalar.activation(o[:, u, :], ps[:, 7, u * P:(u + 1) * P], ACT.Copy, scale=rstd[:, 2 + u:3 + u])
                ins.then_inc(sem["o_scaled"], 1)
                split_hi(2, q1, q2, d2)
                act.wait_ge(sem["oT_turned"], h1)
                nc.scalar.activation(oT[:, 0, bass.ds(h, 1), :], ps[:, 6:7, 0:S], ACT.Copy, scale=gain[:, 0:1]).then_inc(sem["oT_hi"], 1)
                copy_half(1, 3, q1)
                tanh(1)

            for c in YP_PARTS:
                nc.scalar.activation(yp[:, 0, c, :], pooled[:, c, :], ACT.Copy).then_inc(sem["yp_hi"], 1)
            def branch_quad(q, before_last=None):
                q1, q2, d1, d2 = quad_values(act, q)
                n, m = value(act, q - 1), value(act, q - Q_BRANCH + 1)
                split_hi(3, q, q1, d1)
                act.wait_ge(bank_free[2], m)
                copy_half(0, 0, q1)
                split_hi(0, q1, q2, d2)
                act.wait_ge(bank_free[3], m)
                copy_half(1, 1, q1)
                split_hi(1, q1, q2, d2)
                act.wait_ge(bank_free[0], n)
                copy_half(2, 2, q1)
                split_hi(2, q1, q2, d2)
                if before_last:
                    before_last()
                act.wait_ge(bank_free[1], n)
                copy_half(3, 3, q1)

            def chunk_hi(slot, src, scale):
                return nc.scalar.activation(chunk[:, slot:slot + 1, 0, :], src, ACT.Copy, scale=scale)

            def first_chunks(src, scale):
                for slot in range(3):
                    chunk_hi(slot, src[:, slot:slot + 1, :], scale).then_inc(sem["first_hi"], 1)

            def row_phase(src, scale, first, last, ready):
                act.wait_ge(*ready)
                with act.Fori(first, last - 1) as q:
                    q1, q2, d1, d2 = act.snap(q + 1), act.snap(q + 2), act.snap(q * 16 + 16), act.snap(q * 16 + 32)
                    k = [act.snap((q - first) * SLOTS + 3 + s) for s in range(SLOTS)]
                    for i, slot in enumerate((3, 0, 1, 2)):
                        act.wait_ge(w_used[slot], q if slot == 3 else q1)
                        chunk_hi(slot, src[:, bass.ds(k[i], 1), :], scale)
                        if slot == 3:
                            split_hi(3, q, q1, d1)
                        else:
                            split_hi(slot, q1, q2, d2)
                act.wait_ge(w_used[3], last - 1)
                chunk_hi(3, src[:, SLOTS * (last - first) - 1:SLOTS * (last - first), :], scale)
                splits(last - 1, [3])

            with act.Fori(Q_BRANCH, Q_OUT - 1) as q:
                branch_quad(q)
            branch_quad(Q_OUT - 1, before_last=lambda: first_chunks(merged, 0.5))
            row_phase(merged, 0.5, Q_OUT, Q_UP, (sem["merged_ready"], 8))

            def square(src, col, done, out_to):
                nc.scalar.activation(out_to, src, ACT.Square, accum_out=ss[:, col:col + 1]).then_inc(sem[done], 1)

            def square_y(u, b, col, name, last):
                if 4 * u + b < 7:
                    act.wait_ge(sem[f"{name}_done"], 4 * u + b + 1)
                else:
                    act.wait_ge(w_used[3], last)
                square(ps[:, 4 * u + b, :], col + 4 * u + b, f"{name}_squared", junk2[:, (4 * u + b) % 4 * WB:((4 * u + b) % 4 + 1) * WB])

            def x1T_hi(u, b):
                act.wait_ge(sem["x1_turned"], 4 * u + b + 1)
                nc.scalar.activation(xT[:, 0, 4 * b:4 * b + 4, u * P:(u + 1) * P], ps[:, 4 * u + b, :].rearrange("p (k s) -> p k s", k=4),
                                     ACT.Copy).then_inc(sem["x1T_hi"], 1)

            for b in range(4):
                square_y(0, b, 4, "y", Q_UP)
            splits(Q_UP, [0, 1])
            x1T_hi(0, 0)
            x1T_hi(0, 1)
            act.wait_ge(sem["y_squared"], 4)
            for b in range(4):
                square_y(1, b, 4, "y", Q_UP)
            x1T_hi(0, 2)
            x1T_hi(0, 3)
            act.wait_ge(sem["y_squared"], 8)
            act.wait_ge(sem["x1_ready"], 4)
            square(xrow[:, 0, :], 0, "x1_squared", junk2[:, :])
            x1T_hi(1, 0)
            x1T_hi(1, 1)
            splits(Q_UP, [2])
            x1T_hi(1, 2)
            act.wait_ge(sem["x1_ready"], 8)
            act.wait_ge(sem["x1_squared"], 1)
            square(xrow[:, 1, :], 1, "x1_squared", junk2[:, :])
            x1T_hi(1, 3)

            def up_quad(q, is_first=False, before_last=None):
                q1, q2, d1, d2 = quad_values(act, q)
                n, g4 = value(act, q - 11), value(act, (q - Q_UP) * 4 + (4 + GATED0))

                def taps(g):
                    act.wait_ge(z_scaled[g], n)
                    for j in range(2):
                        ft = value(act, (q - Q_UP) * 2 + (FC * g + j))
                        ins = nc.scalar.activation(tmp[g][:, j, :], z[g][:, j, 1:S + 1], ACT.Identity,
                                                   bias=column("conv_b", ft), scale=column("w1", ft))
                    ins.then_inc(sem[f"tap{g}"], 1)

                split_hi(3, q, q1, d1)
                split_hi(0, q1, q2, d2)
                if is_first:
                    copy_R(2)
                copy_half(0, 1, q1)
                split_hi(1, q1, q2, d2)
                taps(0)
                split_hi(2, q1, q2, d2)
                act.wait_ge(sem["gated0"], g4)
                nc.scalar.activation(G[:, :, :], tmp[0][:, :, :], ACT.Gelu_apprx_tanh).then_inc(sem["gelu_ready"], 1)
                if before_last:
                    before_last()
                copy_half(1, 3, q1)
                taps(1)

            act.wait_ge(sem["conv_loaded"], 16)
            up_quad(Q_UP, is_first=True)
            with act.Fori(Q_UP + 1, Q_DOWN - 1) as q:
                up_quad(q)
            up_quad(Q_DOWN - 1, before_last=lambda: first_chunks(hidden, 1.0))
            row_phase(hidden, 1.0, Q_DOWN, Q_END, (sem["act_ready"], Q_DOWN - Q_UP))
            for u in range(TT):
                if u:
                    act.wait_ge(sem["y2_squared"], 4)
                for b in range(4):
                    square_y(u, b, 12, "y2", Q_END)
                act.wait_ge(sem["y2_gained"], 4 * u + 1)
                act.wait_ge(sem["y2_rstd"], u + 1)
                nc.scalar.activation(ybuf[:, u, 0:WB], ybuf[:, u, 0:WB], ACT.Copy, scale=rstd[:, 6 + u:7 + u]).then_inc(sem["y2_scaled"], 1)

        @block.vector
        def _(dve):
            def split_lo(slot, q1):
                dve.wait_ge(w_hi_ready[slot], q1)
                nc.vector.tensor_tensor(w_lo[slot][:, :], w_raw[slot][:, :], w_hi[slot][:, :].bitcast(F32),
                                        ALU.subtract).then_inc(w_lo_ready[slot], 1)

            def sum_halves(g, n):
                dve.wait_ge(half_copied[g], n)
                nc.vector.tensor_tensor(zt(g % 2), pair(g, 0), tmp[g % 2][:, :, :], ALU.add).then_inc(bank_free[g], 1)

            def scale_tokens(g, n, dst):
                dve.wait_ge(bank_free[g], n)
                return nc.vector.tensor_tensor(dst, zt(g), R[:, :, :].to_broadcast([P, 2, S]), ALU.mult)

            nc.vector.memset(ones[:, :], 1.0).then_inc(sem["ones_set"], 1)
            for g in range(2):
                nc.vector.memset(z[g][:, :, :], 0.0).then_inc(sem["ones_set"], 1)

            def turn_lo(c):
                dve.wait_ge(sem["xT_hi"], c - c % 2 + 2)
                src = ps[:, turn_bank(c), (c % 2) * S:(c % 2 + 1) * S]
                nc.vector.scalar_tensor_tensor(xT[:, 1, c, :], src, column("g_pre_mix", c), xT[:, 0, c, :].bitcast(F32),
                                               ALU.mult, ALU.subtract).then_inc(sem["xT_lo"], 1)

            H = PIECE // 2
            for c in range(4):
                turn_lo(c)
            dve.wait_ge(sem["first_w_hi"], 1)
            nc.vector.tensor_tensor(w_lo[0][:, 0:H], w_raw[0][:, 0:H], w_hi[0][:, 0:H].bitcast(F32), ALU.subtract).then_inc(sem["first_w_lo"], 1)
            for c in range(4, 8):
                turn_lo(c)
            dve.wait_ge(w_hi_ready[0], 1)
            nc.vector.tensor_tensor(w_lo[0][:, H:], w_raw[0][:, H:], w_hi[0][:, H:].bitcast(F32), ALU.subtract).then_inc(w_lo_ready[0], 1)
            for c in range(8, KC):
                turn_lo(c)
            dve.wait_ge(sem["first_w_hi"], 2)
            nc.vector.tensor_tensor(w_lo[1][:, 0:H], w_raw[1][:, 0:H], w_hi[1][:, 0:H].bitcast(F32), ALU.subtract).then_inc(sem["first_w_lo"], 1)
            dve.wait_ge(w_hi_ready[1], 1)
            nc.vector.tensor_tensor(w_lo[1][:, H:], w_raw[1][:, H:], w_hi[1][:, H:].bitcast(F32), ALU.subtract).then_inc(w_lo_ready[1], 1)

            def variance(squared, n, col, width, size, eps, done):
                dve.wait_ge(sem[squared], n)
                nc.vector.tensor_scalar(var[:, col:col + width], ss[:, col:col + width], 1.0 / size, eps,
                                        ALU.mult, ALU.add).then_inc(sem[done], 1)

            def diagonal(rstd_ready):
                dve.wait_ge(sem[rstd_ready], 1)
                for u in range(TT):
                    ins = nc.vector.tensor_scalar(diag[:, u * P:(u + 1) * P], ident, rstd[:, u:u + 1], None, ALU.mult)
                ins.then_inc(sem["diag_ready"], 1)

            split_lo(2, 1)
            variance("x_squared", TT, 0, 2, D, EPS, "x_var")
            dve.wait_ge(sem["ones_set"], 3)
            diagonal("x_rstd")
            dve.wait_ge(sem["lam_loaded"], 16)
            nc.vector.tensor_tensor(lamp[:, :, :], lamv[:, :, 0, :], lamv[:, :, 1, :], ALU.mult).then_inc(sem["lam_prod"], 1)
            dve.wait_ge(sem["lam_prod"], 1)
            nc.vector.tensor_reduce(lsum, lamp[:, :, :], AX.X, ALU.add).then_inc(sem["lam_sum"], 1)

            for q in range(Q_V):
                split_lo(3, q + 1)
                split_lo(0, q + 2)
                for g in range(2):
                    if g:
                        split_lo(1, q + 2)
                        split_lo(2, q + 2)
                    sum_halves(g, q + 1)
                    if q == 0:
                        dve.wait_ge(sem["R_ready"], 1)
                    if q < Q_P:
                        tile = 4 * (q % 2) + 2 * g
                        scale_tokens(g, q + 1, qk[:, q // 2, tile:tile + 2, :]).then_inc(z_scaled[g], 1)
                    else:
                        tile = 4 * (q - Q_P) + 2 * g
                        scale_tokens(g, q + 1, ppad[:, tile:tile + 2, PAD:PAD + S]).then_inc(sem["p_ready"], 1)
                if q == 0:
                    dve.wait_ge(sem["lam_exp"], 1)
                    nc.vector.scalar_tensor_tensor(lam, lexp[:, 0:1], LAMBDA_INIT, lexp[:, 1:2], ALU.add, ALU.subtract).then_inc(sem["lam_ready"], 1)
            for q in range(Q_V, Q_GATE):
                split_lo(3, q + 1)
                for slot in range(3):
                    split_lo(slot, q + 2)

            dve.wait_ge(sem["lam_ready"], 1)
            dve.wait_ge(sem["dist_loaded"], 16)
            with dve.Fori(Q_GATE, Q_BRANCH) as q:
                q1, q2, n, h, h1 = dve.snap(q + 1), dve.snap(q + 2), dve.snap(q - 1), dve.snap(q - Q_GATE), dve.snap(q - Q_GATE + 1)
                hu = [dve.snap((q - Q_GATE) * 2 + (1 + u)) for u in range(TT)]
                dve.wait_ge(sem["scores_done"], h1)
                for u in range(TT):
                    nc.vector.scalar_tensor_tensor(t[u][:, :, :], dist[:, u, :, :].to_broadcast([P, 2, S]),
                                                   cst[:, bass.ds(dve.snap(h + C_SLOPE), 1)], ps[:, 4:6, u * S:(u + 1) * S],
                                                   ALU.mult, ALU.add).then_inc(sem["t_biased"], 1)
                    dve.wait_ge(sem["t_biased"], hu[u])
                    nc.vector.tensor_reduce(rmax[:, u, :], t[u][:, :, :], AX.X, ALU.max).then_inc(sem["t_max"], 1)
                    dve.wait_ge(sem["t_max"], hu[u])
                    nc.vector.tensor_scalar(nmax[:, u, :], rmax[:, u, :], -SCALE, None, ALU.mult).then_inc(sem["neg_max"], 1)
                for u in range(TT):
                    dve.wait_ge(sem["exp_done"], hu[u])
                    nc.vector.reciprocal(einv[:, u, :], esum[:, u, :]).then_inc(sem["sum_inv"], 1)
                    dve.wait_ge(sem["sum_inv"], hu[u])
                    nc.vector.tensor_scalar(linv[:, u:u + 1], einv[:, u, 1:2], lam, None, ALU.mult).then_inc(sem["lam_inv"], 1)
                    dve.wait_ge(sem["lam_inv"], hu[u])
                    nc.vector.tensor_scalar(t[u][:, 1, :], t[u][:, 1, :], linv[:, u:u + 1], None, ALU.mult).then_inc(sem["p1_scaled"], 1)
                    dve.wait_ge(sem["p1_scaled"], hu[u])
                    nc.vector.scalar_tensor_tensor(probs[:, u, :], t[u][:, 0, :], einv[:, u, 0:1], t[u][:, 1, :],
                                                   ALU.mult, ALU.subtract).then_inc(sem["probs_ready"], 1)
                split_lo(3, q1)
                split_lo(0, q2)
                dve.wait_ge(sem["pT_turned"], h1)
                nc.vector.tensor_copy(pT[:, :, :], ps[:, 6, :].rearrange("p (k s) -> p k s", k=TT)).then_inc(sem["pT_ready"], 1)
                sum_halves(0, n)
                scale_tokens(0, n, zt(0)).then_inc(z_scaled[0], 1)
                split_lo(1, q2)
                dve.wait_ge(sem["o_squared"], h1)
                nc.vector.tensor_scalar(var[:, 2:4], ss[:, 2:4], 1.0 / P, SUBLN_EPS, ALU.mult, ALU.add).then_inc(sem["o_var"], 1)
                split_lo(2, q2)
                dve.wait_ge(sem["oT_hi"], h1)
                nc.vector.scalar_tensor_tensor(oT[:, 1, bass.ds(h, 1), :], ps[:, 6:7, 0:S], gain[:, 0:1],
                                               oT[:, 0, bass.ds(h, 1), :].bitcast(F32), ALU.mult, ALU.subtract).then_inc(sem["oT_lo"], 1)
                sum_halves(1, n)
                scale_tokens(1, n, zt(1)).then_inc(z_scaled[1], 1)

            for i, c in enumerate(YP_PARTS):
                dve.wait_ge(sem["yp_hi"], i + 1)
                nc.vector.tensor_tensor(yp[:, 1, c, :], pooled[:, c, :], yp[:, 0, c, :].bitcast(F32), ALU.subtract).then_inc(sem["yp_lo"], 1)
            dve.wait_ge(sem["gate_ready"], 16)
            def branch_quad(q, before_last=None):
                q1, q2 = value(dve, q + 1), value(dve, q + 2)
                n, m = value(dve, q - 1), value(dve, q - Q_BRANCH + 1)
                m1 = value(dve, q - Q_BRANCH + 2)
                a1 = [value(dve, (q - Q_BRANCH) * 2 + (1 + s)) for s in range(2)]

                def gate(g, count, tile, done):
                    dve.wait_ge(bank_free[g], count)
                    nc.vector.scalar_tensor_tensor(zt(g % 2), gates[:, bass.ds(tile, 2), :], 1.0, zt(g % 2),
                                                   ALU.add, ALU.mult).then_inc(sem[f"gated{g % 2}"], 1)
                    dve.wait_ge(sem[f"gated{g % 2}"], done)

                for s in range(2):
                    split_lo(3 if s == 0 else 1, q1 if s == 0 else q2)
                    tile = value(dve, (q - Q_BRANCH) * 4 + 2 * s)
                    tile2 = value(dve, (q - Q_BRANCH) * 4 + (2 * s + KC))
                    sum_halves(2 * s, n if s == 0 else m)
                    gate(2 * s, n if s == 0 else m1, tile, a1[s])
                    if s and before_last:
                        before_last()
                    split_lo(2 * s, q2)
                    sum_halves(2 * s + 1, n if s == 0 else m)
                    gate(2 * s + 1, n if s == 0 else m1, tile2, a1[s])
                    nc.vector.tensor_tensor(merged[:, bass.ds(tile, 2), :], zt(0), zt(1), ALU.add).then_inc(sem["merged_ready"], 1)
                    dve.wait_ge(sem["merged_ready"], a1[s])

            def chunk_lo(slot, src, scale):
                return nc.vector.scalar_tensor_tensor(chunk[:, slot:slot + 1, 1, :], src, scale, chunk[:, slot:slot + 1, 0, :].bitcast(F32),
                                                      ALU.mult, ALU.subtract)

            def first_chunks(src, scale, done):
                for slot in range(3):
                    dve.wait_ge(sem["first_hi"], done + slot + 1)
                    chunk_lo(slot, src[:, slot:slot + 1, :], scale).then_inc(sem["first_lo"], 1)

            def row_phase(src, scale, first, last):
                with dve.Fori(first, last - 1) as q:
                    q1, q2 = dve.snap(q + 1), dve.snap(q + 2)
                    k = [dve.snap((q - first) * SLOTS + 3 + s) for s in range(SLOTS)]
                    for i, slot in enumerate((3, 0, 1, 2)):
                        dve.wait_ge(w_hi_ready[slot], q1 if slot == 3 else q2)
                        chunk_lo(slot, src[:, bass.ds(k[i], 1), :], scale)
                        split_lo(slot, q1 if slot == 3 else q2)
                dve.wait_ge(w_hi_ready[3], last)
                chunk_lo(3, src[:, SLOTS * (last - first) - 1:SLOTS * (last - first), :], scale)
                split_lo(3, last)

            with dve.Fori(Q_BRANCH, Q_OUT - 1) as q:
                branch_quad(q)
            branch_quad(Q_OUT - 1, before_last=lambda: first_chunks(merged, 0.5, 0))
            row_phase(merged, 0.5, Q_OUT, Q_UP)

            def gain_y(u, b, name):
                dve.wait_ge(sem[f"{name}_squared"], 4 * u + b + 1)
                nc.vector.tensor_tensor(ybuf[:, u, WB * b:WB * (b + 1)], ps[:, 4 * u + b, :], grow[:, WB * b:WB * (b + 1)],
                                        ALU.mult).then_inc(sem[f"{name}_gained"], 1)

            def row_factor(u, col, name, before):
                for b in range(before):
                    gain_y(u, b, name)
                dve.wait_ge(sem[f"{name}_squared"], 4 * u + 4)
                at = ysum[:, (col // 12) * 2 + u:(col // 12) * 2 + u + 1]
                nc.vector.tensor_reduce(at, ss[:, col + 4 * u:col + 4 * u + 4], AX.X, ALU.add).then_inc(sem[f"{name}_summed"], 1)
                dve.wait_ge(sem[f"{name}_summed"], u + 1)
                r = 4 + (col // 12) * 2 + u
                nc.vector.tensor_scalar(var[:, r:r + 1], at, 1.0 / D, EPS, ALU.mult, ALU.add).then_inc(sem[f"{name}_var"], 1)
                for b in range(before, 4):
                    gain_y(u, b, name)
                dve.wait_ge(sem[f"{name}_rstd"], u + 1)
                return rstd[:, r:r + 1]

            def add_x(u, b, factor, name, done):
                dve.wait_ge(sem[f"{name}_gained"], 4 * u + b + 1)
                nc.vector.scalar_tensor_tensor(xrow[:, u, WB * b:WB * (b + 1)], ybuf[:, u, WB * b:WB * (b + 1)], factor,
                                               xrow[:, u, WB * b:WB * (b + 1)], ALU.mult, ALU.add).then_inc(sem[done], 1)

            def x1T_lo(u, b):
                dve.wait_ge(sem["x1T_hi"], 4 * u + b + 1)
                nc.vector.tensor_tensor(xT[:, 1, 4 * b:4 * b + 4, u * P:(u + 1) * P], ps[:, 4 * u + b, :].rearrange("p (k s) -> p k s", k=4),
                                        xT[:, 0, 4 * b:4 * b + 4, u * P:(u + 1) * P].bitcast(F32), ALU.subtract).then_inc(sem["x1T_lo"], 1)

            dve.wait_ge(sem["xrow_loaded"], 16)
            dve.wait_ge(sem["grow_loaded"], 16)
            factor = row_factor(0, 4, "y", 3)
            for b in range(4):
                add_x(0, b, factor, "y", "x1_ready")
            split_lo(0, Q_UP + 1)
            x1T_lo(0, 0)
            x1T_lo(0, 1)
            split_lo(1, Q_UP + 1)
            factor = row_factor(1, 4, "y", 2)
            add_x(1, 0, factor, "y", "x1_ready")
            dve.wait_ge(sem["x1_ready"], 5)
            dve.wait_ge(sem["g2row_loaded"], 16)
            nc.vector.tensor_tensor(ybuf[:, 1, 0:WB], xrow[:, 1, 0:WB], g2row[:, 0:WB], ALU.mult).then_inc(sem["x1g_first"], 1)
            x1T_lo(0, 2)
            add_x(1, 1, factor, "y", "x1_ready")
            x1T_lo(0, 3)
            add_x(1, 2, factor, "y", "x1_ready")
            x1T_lo(1, 0)
            add_x(1, 3, factor, "y", "x1_ready")
            x1T_lo(1, 1)
            x1T_lo(1, 2)
            split_lo(2, Q_UP + 1)
            x1T_lo(1, 3)
            variance("x1_squared", TT, 0, 2, D, EPS, "x1_var")
            diagonal("x1_rstd")

            def up_quad(q, is_first=False, before_last=None):
                q1, q2, n, i1 = value(dve, q + 1), value(dve, q + 2), value(dve, q - 5), value(dve, q - Q_UP + 1)
                taps_done = [value(dve, (q - Q_UP) * 4 + (GATED0 + k)) for k in (1, 3, 4)]

                def conv(g):
                    dve.wait_ge(sem[f"tap{g}"], i1)
                    done = sem[f"gated{g}"]
                    for j in range(2):
                        ft = value(dve, (q - Q_UP) * 2 + (FC * g + j))
                        nc.vector.scalar_tensor_tensor(tmp[g][:, j, :], z[g][:, j, 0:S], column("w0", ft), tmp[g][:, j, :],
                                                       ALU.mult, ALU.add).then_inc(done, 1)
                        dve.wait_ge(done, taps_done[j])
                        nc.vector.scalar_tensor_tensor(tmp[g][:, j, :], z[g][:, j, 2:S + 2], column("w2", ft), tmp[g][:, j, :],
                                                       ALU.mult, ALU.add).then_inc(done, 1)

                split_lo(3, q1)
                split_lo(0, q2)
                sum_halves(0, n)
                if is_first:
                    dve.wait_ge(sem["R_ready"], 2)
                scale_tokens(0, n, zt(0)).then_inc(z_scaled[0], 1)
                split_lo(1, q2)
                conv(0)
                split_lo(2, q2)
                if before_last:
                    before_last()
                sum_halves(1, n)
                scale_tokens(1, n, zt(1)).then_inc(z_scaled[1], 1)
                conv(1)
                dve.wait_ge(sem["gated1"], taps_done[2])
                dve.wait_ge(sem["gelu_ready"], i1)
                tile = value(dve, (q - Q_UP) * 2)
                nc.vector.tensor_tensor(hidden[:, bass.ds(tile, 2), :], G[:, :, :], tmp[1][:, :, :], ALU.mult).then_inc(sem["act_ready"], 1)

            dve.wait_ge(sem["conv_loaded"], 16)
            up_quad(Q_UP, is_first=True)
            with dve.Fori(Q_UP + 1, Q_DOWN - 1) as q:
                up_quad(q)
            up_quad(Q_DOWN - 1, before_last=lambda: first_chunks(hidden, 1.0, 3))
            dve.wait_ge(sem["act_ready"], Q_DOWN - Q_UP)
            row_phase(hidden, 1.0, Q_DOWN, Q_END)
            dve.wait_ge(sem["grow2_loaded"], 16)
            for u in range(TT):
                factor = row_factor(u, 12, "y2", 3)
                for b in range(1, 4):
                    add_x(u, b, factor, "y2", "out_ready")

        @block.tensor
        def _(pe):
            def ready(slot, q1):
                pe.wait_ge(w_hi_ready[slot], q1)
                pe.wait_ge(w_lo_ready[slot], q1)

            def column_piece(slot, q1, g, moving, c0, last, first=True, half=None, chunk_wait=None):
                if half != 0:
                    ready(slot, q1)
                for k in range(GK) if half is None else range(4 * half, 4 * half + 4):
                    c = c0 + k
                    if chunk_wait:
                        chunk_wait(c)
                    for j in range(2):
                        col = slice(k * S + j * P, k * S + (j + 1) * P)
                        nc.tensor.matmul(ps[:, 2 * g + j, :].rearrange("p (a s) -> p a s", a=2), w_hi[slot][:, col], moving[:, :, c, :],
                                         start=(k == 0 and first), stop=False, skip_group_check=True)
                        ins = nc.tensor.matmul(ps[:, 2 * g + j, 0:S], w_lo[slot][:, col], moving[:, 0, c, :],
                                               start=False, stop=(k == GK - 1 and last), skip_group_check=True)
                if half != 0:
                    ins.then_inc(w_used[slot], 1)

            def token_piece(slot, u, moving_of, stationary_of, bank_of, groups, first, last, before=None):
                for w, hl in ((w_hi, 0), (w_lo, 0), (w_hi, 1)):
                    for g in range(groups):
                        if before and w is w_hi and hl == 0:
                            before(g)
                        ins = nc.tensor.matmul(ps[:, bank_of(g), :], stationary_of(hl), moving_of(w, g),
                                               start=(first and w is w_hi and hl == 0), stop=(last and hl == 1),
                                               skip_group_check=True)
                return ins

            def turn_x(i):
                pe.wait_ge(sem[f"x_loaded{i}"], 16)
                if i == 3:
                    pe.wait_ge(sem["xT_lo"], 4)
                for k in range(4):
                    for u in range(TT):
                        ins = nc.tensor.transpose(ps[:, turn_bank(4 * i + k), (k % 2) * S + u * P:(k % 2) * S + (u + 1) * P],
                                                  xs[:, u, (4 * i + k) * P:(4 * i + k + 1) * P], ident)
                ins.then_inc(sem["xT_turned"], 1)

            def spread_R():
                nc.tensor.matmul(ps[:, 7, 0:S], ones[:, :], diag, start=True, stop=True).then_inc(sem["R_summed"], 1)

            pe.wait_ge(sem["ident_loaded"], 16)
            for i in range(4):
                turn_x(i)
            pe.wait_ge(sem["first_w_lo"], 1)
            column_piece(0, 1, 0, xT, 0, False, half=0)
            pe.wait_ge(sem["xT_lo"], 8)
            column_piece(0, 1, 0, xT, 0, False, half=1)
            pe.wait_ge(sem["xT_lo"], KC)
            column_piece(1, 1, 0, xT, GK, True, first=False)
            column_piece(2, 1, 1, xT, 0, False)
            pe.wait_ge(sem["diag_ready"], 1)
            spread_R()
            column_piece(3, 1, 1, xT, GK, True, first=False)
            with pe.Fori(1, Q_V) as q:
                q1 = pe.snap(q + 1)
                for g in range(2):
                    pe.wait_ge(bank_free[g], q)
                    column_piece(2 * g, q1, g, xT, 0, False)
                    column_piece(2 * g + 1, q1, g, xT, GK, True, first=False)

            for q in range(Q_V, Q_GATE):
                pe.wait_ge(bank_free[q - Q_V], Q_V)
                for slot in range(SLOTS):
                    if q == Q_GATE - 1 and slot == 2:
                        pe.wait_ge(sem["poolw_loaded"], 16)
                        for grp in range(4):
                            pe.wait_ge(sem["mixed_ready"], grp + 1)
                            for j in range(2):
                                for k in range(2):
                                    ins = nc.tensor.matmul(ps[:, 4 + grp, j * S:(j + 1) * S], pw[:, grp, k, j * P:(j + 1) * P],
                                                           mixed[:, 2 * grp + k, :], start=(k == 0), stop=(k == 1), skip_group_check=True)
                            ins.then_inc(sem["pooled"], 1)
                    ready(slot, q + 1)
                    for k in range(4):
                        c = 4 * slot + k
                        for u in range(TT):
                            ins = token_piece(slot, u, lambda w, g: w[slot][:, WB * k:WB * (k + 1)],
                                              lambda hl: xT[:, hl, c, u * P:(u + 1) * P],
                                              lambda g: 2 * (q - Q_V) + u, 1, c == 0, c == KC - 1)
                    ins.then_inc(w_used[slot], 1)

            pe.wait_ge(bank_free[2], 1)
            pe.wait_ge(bank_free[3], 1)
            with pe.Fori(Q_GATE, Q_BRANCH) as q:
                q1, nf, h1 = pe.snap(q + 1), pe.snap(q - 2), pe.snap(q - Q_GATE + 1)
                hu2 = pe.snap((q - Q_GATE) * 2 + 2)
                pe.wait_ge(sem["head_qk"], h1)
                for c in range(2):
                    rows = slice(c * HD, (c + 1) * HD)
                    for u in range(TT):
                        for q_part, k_part in ((0, 0), (0, 1), (1, 0)):
                            ins = nc.tensor.matmul(ps[:, 4 + c, u * S:(u + 1) * S], qk_head[rows, q_part, 0, u * P:(u + 1) * P],
                                                   qk_head[rows, k_part, 1, :], start=(q_part + k_part == 0), stop=(q_part == 1),
                                                   skip_group_check=True)
                ins.then_inc(sem["scores_done"], 1)
                pe.wait_ge(sem["v_ready"], 2)
                pe.wait_ge(bank_free[0], nf)
                column_piece(0, q1, 0, xT, 0, False)
                column_piece(1, q1, 0, xT, GK, True, first=False)
                pe.wait_ge(sem["probs_ready"], hu2)
                for u in range(TT):
                    for k in range(TT):
                        ins = nc.tensor.transpose(ps[:, 6, k * S + u * P:k * S + (u + 1) * P], probs[:, u, k * P:(k + 1) * P], ident)
                ins.then_inc(sem["pT_turned"], 1)
                pe.wait_ge(sem["v_ready"], 4)
                pe.wait_ge(bank_free[1], nf)
                column_piece(2, q1, 1, xT, 0, False)
                pe.wait_ge(sem["pT_ready"], h1)
                pe.wait_ge(sem["head_v"], h1)
                for u in range(TT):
                    for k in range(TT):
                        ins = nc.tensor.matmul(ps[:, 7, u * P:(u + 1) * P], pT[:, k, u * P:(u + 1) * P], v_head[:, k, :],
                                               start=(k == 0), stop=(k == TT - 1), skip_group_check=True)
                ins.then_inc(sem["o_done"], 1)
                column_piece(3, q1, 1, xT, GK, True, first=False)
                pe.wait_ge(sem["o_scaled"], h1)
                for u in range(TT):
                    ins = nc.tensor.transpose(ps[:, 6, u * P:(u + 1) * P], o[:, u, :], ident)
                ins.then_inc(sem["oT_turned"], 1)

            def head_ready(c):
                if c in (0, HEADS - 1):
                    pe.wait_ge(sem["oT_lo"], HEADS - (c == 0))

            def pooled_ready(c):
                if c % 2 == 0:
                    pe.wait_ge(sem["yp_lo"], 1 + c // 2)

            with pe.Fori(Q_BRANCH, Q_OUT) as q:
                q1, nf, mf = pe.snap(q + 1), pe.snap(q - 2), pe.snap(q - Q_BRANCH + 1)
                for g in range(4):
                    pe.wait_ge(bank_free[g], nf if g < 2 else mf)
                    column_piece(g, q1, g, yp if g % 2 else oT, 0, True, chunk_wait=pooled_ready if g % 2 else head_ready)

            def row_piece(slot, u, first, last, before=None):
                return token_piece(slot, u, lambda w, g: w[slot][:, WB * g:WB * (g + 1)],
                                   lambda hl: chunk[:, slot, hl, u * P:(u + 1) * P],
                                   lambda g: 4 * u + g, 4, first, last, before)

            def row_phase(first, last, done, order, bank_wait, first_chunks, between=None):
                def quad(q1, is_first):
                    for slot in range(SLOTS):
                        ready(slot, q1)
                        if is_first and slot < 3:
                            pe.wait_ge(sem["first_lo"], first_chunks + slot + 1)
                        for u in order:
                            ins = row_piece(slot, u, is_first and slot == 0, False,
                                            before=(lambda g: bank_wait(u, g)) if is_first and slot == 0 else None)
                        ins.then_inc(w_used[slot], 1)

                quad(first + 1, True)
                with pe.Fori(first + 1, last - 1) as q:
                    quad(pe.snap(q + 1), False)
                for u in range(TT):
                    for slot in range(SLOTS):
                        if u == 0:
                            ready(slot, last)
                        if between and u == 1 and slot >= 2:
                            between(slot)
                        if slot < 3:
                            ins = row_piece(slot, u, False, False)
                            if u == 1:
                                ins.then_inc(w_used[slot], 1)
                        else:
                            for g in range(4):
                                for w, hl in ((w_hi, 0), (w_lo, 0), (w_hi, 1)):
                                    ins = nc.tensor.matmul(ps[:, 4 * u + g, :], chunk[:, slot, hl, u * P:(u + 1) * P],
                                                           w[slot][:, WB * g:WB * (g + 1)], start=False, stop=(hl == 1),
                                                           skip_group_check=True)
                                if u == 1 and g == 3:
                                    ins.then_inc(w_used[slot], 1)
                                else:
                                    ins.then_inc(done, 1)

            def turn_x1(u, b):
                if (u, b) == (1, 0):
                    pe.wait_ge(sem["x1g_first"], 1)
                else:
                    pe.wait_ge(sem[f"x1g_ready{u}"], b + 1 - u)
                for k in range(4):
                    c = 4 * b + k
                    ins = nc.tensor.transpose(ps[:, 4 * u + b, k * P:(k + 1) * P], ybuf[:, u, c * P:(c + 1) * P], ident)
                ins.then_inc(sem["x1_turned"], 1)

            def after_branches(u, g):
                if g % 2 == 0:
                    grp = 2 * u + g // 2
                    pe.wait_ge(bank_free[grp], 18 if grp < 2 else 5)

            row_phase(Q_OUT, Q_UP, sem["y_done"], (0, 1), after_branches, 0,
                      between=lambda slot: [turn_x1(0, b) for b in ((0, 1) if slot == 2 else (2,))])
            turn_x1(0, 3)

            def tile_piece(slot, u, c0, first, last):
                def product(w, out, moving, start=False, stop=False):
                    return nc.tensor.matmul(out, w[slot][:, col], moving, start=start, stop=stop, skip_group_check=True)

                for k in range(GK):
                    c = c0 + k
                    if c % 4 == 0:
                        pe.wait_ge(sem["x1T_lo"], max(4 * u + c // 4 + 1, 2))
                        if u and c < 3 * 4:
                            turn_x1(1, c // 4 + 1)
                    for j in range(2):
                        col = slice(k * S + j * P, k * S + (j + 1) * P)
                        tile_out = ps[:, j, :].rearrange("p (a s) -> p a s", a=2)[:, :, u * P:(u + 1) * P]
                        tile_in = xT[:, :, c, u * P:(u + 1) * P]
                        product(w_hi, tile_out, tile_in, start=(first and u == 0 and k == 0))
                        if not last:
                            ins = product(w_lo, tile_out, tile_in)
                        elif u:
                            ins = product(w_lo, ps[:, j, 0:S], xT[:, 0, c, :], stop=(k == GK - 1))
                if u:
                    ins.then_inc(w_used[slot], 1)

            ready(0, Q_UP + 1)
            tile_piece(0, 0, 0, True, False)
            turn_x1(1, 0)
            ready(1, Q_UP + 1)
            tile_piece(1, 0, GK, False, True)
            tile_piece(0, 1, 0, True, False)
            tile_piece(1, 1, GK, False, True)
            pe.wait_ge(sem["diag_ready"], 2)
            spread_R()
            column_piece(2, Q_UP + 1, 1, xT, 0, False)
            column_piece(3, Q_UP + 1, 1, xT, GK, True, first=False)
            with pe.Fori(Q_UP + 1, Q_DOWN) as q:
                q1, nf = pe.snap(q + 1), pe.snap(q - 6)
                for g in range(2):
                    pe.wait_ge(bank_free[g], nf)
                    column_piece(2 * g, q1, g, xT, 0, False)
                    column_piece(2 * g + 1, q1, g, xT, GK, True, first=False)

            def after_up(u, g):
                if u == 0 and g % 2 == 0:
                    pe.wait_ge(bank_free[g // 2], Q_DOWN - 6)

            row_phase(Q_DOWN, Q_END, sem["y2_done"], (1, 0), after_up, 3)


GATED0 = 8


def kernel(**inputs):
    import numpy as np
    import concourse.bacc as bacc
    from concourse.bass_utils import run_bass_kernel_spmd

    def feature_columns(a):
        return np.ascontiguousarray(a.reshape(-1, P).T)

    g = {k: np.asarray(a) for k, a in inputs.items()}
    conv = g["conv_w"][0]
    params = np.concatenate([feature_columns(a) for a in (
        g["g_pre_mix"][0], g["b_gate"][0], g["pool_scale"][0], g["subln_gain"][0],
        conv[0], conv[1], conv[2], g["conv_b"][0])], axis=1)
    lambdas = np.concatenate([g["lambda_q1"], g["lambda_k1"], g["lambda_q2"], g["lambda_k2"]], axis=1)

    keys = np.arange(S)
    dist = np.abs(np.arange(P)[:, None, None] + P * np.arange(TT)[None, :, None] - keys[None, None, :])
    slopes = np.array([-(2.0 ** (-8.0 * (h + 1) / HEADS)) / SCALE for h in range(HEADS)])
    consts = np.concatenate([np.eye(P), dist.reshape(P, TT * S), np.tile(slopes, (P, 1))], axis=1).astype(np.float32)
    counts = np.stack([np.minimum(keys + w // 2, S) - np.maximum(keys - w // 2, 0) for w in WINDOWS])
    invcnt = np.ascontiguousarray(np.broadcast_to((1.0 / counts).reshape(1, -1), (P, 4 * S)).astype(np.float32))

    arrays = {"x": g["x"][0], "w_in": g["w_in"][0], "w_attn_branch": g["w_attn_branch"][0], "pool_w": g["pool_w"][0],
              "w_pool_branch": g["w_pool_branch"][0], "w_out": g["w_out"][0], "w_up": g["w_up"][0], "w_down": g["w_down"][0],
              "g_post_mix": g["g_post_mix"], "g_pre_ffn": g["g_pre_ffn"], "g_post_ffn": g["g_post_ffn"], "lambdas": lambdas, "params": params,
              "consts": consts, "invcnt": invcnt}
    arrays = {k: np.ascontiguousarray(a) for k, a in arrays.items()}
    nc = bacc.Bacc("TRN2", target_bir_lowering=False, num_devices=1, dynamic_dma_scratch_size=1024)
    args = [nc.dram_tensor(f"in_{k}", a.shape, F32, kind="ExternalInput").ap() for k, a in arrays.items()]
    out = nc.dram_tensor("out", (S, D), F32, kind="ExternalOutput").ap()
    build(nc, *args, out)
    r = run_bass_kernel_spmd(nc, [{f"in_{k}": a for k, a in arrays.items()}], core_ids=[0])
    return r.results[0]["out"].reshape(1, S, D)
```
